# Optimizing a Trainium2 kernel written in Bass

```python
import jax
import jax.numpy as jnp
from jax import lax
import numpy as np

D_MODEL = 1024
BATCH = 1
SEQ = 256
DEPTH = 2

HEAD_DIM = 64
SB_HEADS = D_MODEL // 256
SB_WIDTH = SB_HEADS * HEAD_DIM
CV_WIDTH = D_MODEL // 4
CV_KERNEL = 31
DL_HEADS = D_MODEL // 128
DL_WIDTH = DL_HEADS * HEAD_DIM
MIX_WIDTH = SB_WIDTH + CV_WIDTH + DL_WIDTH
IN_WIDTH = 3 * SB_WIDTH + 2 * CV_WIDTH + 3 * DL_WIDTH
DL_PATTERN = ((128, 1), (512, 4), (2048, 16))
BLOCK = 128
ROPE_THETA = 10000.0
N_MEM = 256
X_HEADS = 4
X_HEAD_DIM = D_MODEL // X_HEADS
D_FF = 2816
FFN_KERNEL = 3
EPS = 1e-6

kernel_name = 'hybrid_stickbreak_conformer_dilated'

def rms_norm(x, g):
    xf = x.astype(jnp.float32)
    y = xf * lax.rsqrt(jnp.mean(xf * xf, axis=-1, keepdims=True) + EPS)
    return (y * g.astype(jnp.float32)).astype(x.dtype)

def layer_norm(x, g, b):
    xf = x.astype(jnp.float32)
    mu = jnp.mean(xf, axis=-1, keepdims=True)
    var = jnp.mean(jnp.square(xf - mu), axis=-1, keepdims=True)
    y = (xf - mu) * lax.rsqrt(var + EPS)
    return (y * g.astype(jnp.float32) + b.astype(jnp.float32)).astype(x.dtype)

def causal_depthwise_conv(x, w, b):
    k_width, ch = w.shape
    y = lax.conv_general_dilated(
        x, w[:, None, :].astype(x.dtype), window_strides=(1,),
        padding=((k_width - 1, 0),), dimension_numbers=('NWC', 'WIO', 'NWC'),
        feature_group_count=ch)
    return y + b.astype(x.dtype)

def rope(x, positions):
    half = x.shape[-1] // 2
    inv_freq = ROPE_THETA ** (-jnp.arange(half, dtype=jnp.float32) / half)
    ang = positions.astype(jnp.float32)[..., None] * inv_freq
    cos = jnp.cos(ang)[:, :, None, :]
    sin = jnp.sin(ang)[:, :, None, :]
    xf = x.astype(jnp.float32)
    x1, x2 = xf[..., :half], xf[..., half:]
    return jnp.concatenate([x1 * cos - x2 * sin, x2 * cos + x1 * sin], axis=-1).astype(x.dtype)

def stick_breaking_attention(q, k, v):
    b_, s_, h_, hd = q.shape
    scale = hd ** -0.5
    qh, kh, vh = (t.transpose(0, 2, 1, 3) for t in (q, k, v))
    outs = []
    for n in range(s_ // BLOCK):
        t0, t1 = n * BLOCK, (n + 1) * BLOCK
        z = jnp.einsum('bhqc,bhkc->bhqk', qh[:, :, t0:t1], kh[:, :, :t1]).astype(jnp.float32) * scale
        t_idx = t0 + jnp.arange(BLOCK)[:, None]
        s_idx = jnp.arange(t1)[None, :]
        before = s_idx < t_idx
        log_keep = jnp.where(before, jax.nn.log_sigmoid(-z), 0.0)
        between = lax.cumsum(log_keep, axis=3, reverse=True) - log_keep
        a = jnp.where(before, jnp.exp(jax.nn.log_sigmoid(z) + between), 0.0)
        outs.append(jnp.einsum('bhqk,bhkc->bhqc', a.astype(vh.dtype), vh[:, :, :t1]))
    o = jnp.concatenate(outs, axis=2)
    return o.transpose(0, 2, 1, 3)

def dilated_branch(q, k, v, window, dilation):
    b_, s_, h_, hd = q.shape
    w_steps = window // dilation
    assert w_steps <= BLOCK
    seq_sub = s_ // dilation
    nb = -(-seq_sub // BLOCK)
    pad_len = nb * BLOCK - seq_sub
    scale = hd ** -0.5

    def to_sub(t):
        t = t.reshape(b_, seq_sub, dilation, h_, hd).transpose(0, 2, 3, 1, 4)
        t = jnp.pad(t, ((0, 0), (0, 0), (0, 0), (0, pad_len), (0, 0)))
        return t.reshape(b_, dilation, h_, nb, BLOCK, hd)

    def with_prev(t):
        prev = jnp.pad(t, ((0, 0), (0, 0), (0, 0), (1, 0), (0, 0), (0, 0)))[:, :, :, :-1]
        return jnp.concatenate([prev, t], axis=4)

    qs = to_sub(q)
    kw = with_prev(to_sub(k))
    vw = with_prev(to_sub(v))
    s = jnp.einsum('brhnqc,brhnkc->brhnqk', qs, kw).astype(jnp.float32) * scale
    qi = jnp.arange(nb)[:, None, None] * BLOCK + jnp.arange(BLOCK)[None, :, None]
    ki = (jnp.arange(nb)[:, None, None] - 1) * BLOCK + jnp.arange(2 * BLOCK)[None, None, :]
    dist = qi - ki
    valid = (dist >= 0) & (dist <= w_steps) & (ki >= 0)
    s = jnp.where(valid, s, -jnp.inf)
    m = jnp.max(s, axis=-1, keepdims=True)
    p = jnp.exp(s - m)
    den = jnp.sum(p, axis=-1, keepdims=True)
    o = jnp.einsum('brhnqk,brhnkc->brhnqc', (p / den).astype(v.dtype), vw)
    lse = (m + jnp.log(den))[..., 0]
    o = o.reshape(b_, dilation, h_, nb * BLOCK, hd)[:, :, :, :seq_sub]
    o = o.transpose(0, 3, 1, 2, 4).reshape(b_, s_, h_, hd)
    lse = lse.reshape(b_, dilation, h_, nb * BLOCK)[:, :, :, :seq_sub]
    lse = lse.transpose(0, 3, 1, 2).reshape(b_, s_, h_)
    return o, lse

def dilated_mixture(q, k, v):
    outs, lses = [], []
    for window, dilation in DL_PATTERN:
        o, lse = dilated_branch(q, k, v, window, dilation)
        outs.append(o)
        lses.append(lse)
    wts = jax.nn.softmax(jnp.stack(lses, axis=-1), axis=-1)
    o = jnp.einsum('bshn,nbshc->bshc', wts, jnp.stack(outs, axis=0).astype(jnp.float32))
    return o.astype(v.dtype)

def conformer_conv(val, gate, cv_w, cv_b, cv_ln_g, cv_ln_b, cv_pw_w, cv_pw_b):
    g = val * jax.nn.sigmoid(gate)
    c = causal_depthwise_conv(g, cv_w, cv_b)
    c = jax.nn.silu(layer_norm(c, cv_ln_g, cv_ln_b))
    return c @ cv_pw_w + cv_pw_b

def hybrid_mixer(h, positions, w_in, cv_w, cv_b, cv_ln_g, cv_ln_b, cv_pw_w, cv_pw_b, w_out):
    b_, s_, _ = h.shape
    u = h @ w_in
    o1 = 3 * SB_WIDTH
    o2 = o1 + 2 * CV_WIDTH
    sb = u[..., :o1].reshape(b_, s_, 3, SB_HEADS, HEAD_DIM)
    cv = u[..., o1:o2]
    dl = u[..., o2:].reshape(b_, s_, 3, DL_HEADS, HEAD_DIM)
    a_out = stick_breaking_attention(sb[:, :, 0], sb[:, :, 1], sb[:, :, 2]).reshape(b_, s_, SB_WIDTH)
    b_out = conformer_conv(cv[..., :CV_WIDTH], cv[..., CV_WIDTH:], cv_w, cv_b, cv_ln_g, cv_ln_b, cv_pw_w, cv_pw_b)
    q = rope(dl[:, :, 0], positions)
    k = rope(dl[:, :, 1], positions)
    c_out = dilated_mixture(q, k, dl[:, :, 2]).reshape(b_, s_, DL_WIDTH)
    return jnp.concatenate([a_out, b_out, c_out], axis=-1) @ w_out

def memory_cross_attention(h, mem_n, wq, wk, wv, wo):
    b_, s_, _ = h.shape
    q = (h @ wq).reshape(b_, s_, X_HEADS, X_HEAD_DIM)
    k = (mem_n @ wk).reshape(b_, -1, X_HEADS, X_HEAD_DIM)
    v = (mem_n @ wv).reshape(b_, -1, X_HEADS, X_HEAD_DIM)
    s = jnp.einsum('bshc,bmhc->bhsm', q, k).astype(jnp.float32) * (X_HEAD_DIM ** -0.5)
    p = jax.nn.softmax(s, axis=-1).astype(v.dtype)
    o = jnp.einsum('bhsm,bmhc->bshc', p, v).reshape(b_, s_, D_MODEL)
    return o @ wo

def conv_ffn(h, w_up, conv_w, conv_b, w_down):
    u = causal_depthwise_conv(h @ w_up, conv_w, conv_b)
    gate, val = u[..., :D_FF], u[..., D_FF:]
    return (jax.nn.gelu(gate, approximate=True) * val) @ w_down

def setup_inputs(seed: int = 0) -> dict:
    key = jax.random.key(seed)
    ks = jax.random.split(key, 32)
    f32 = jnp.float32

    def dense(k, shape, fan_in):
        return jax.random.normal(k, shape, f32) * (fan_in ** -0.5)

    def gain(k, shape):
        return 1.0 + 0.02 * jax.random.normal(k, shape, f32)

    def bias(k, shape):
        return 0.02 * jax.random.normal(k, shape, f32)

    offset = jax.random.randint(ks[2], (BATCH, 1), 0, 1024, dtype=jnp.int32)
    positions = (offset + jnp.arange(SEQ, dtype=jnp.int32)[None, :]).astype(jnp.int32)
    return {
        'x': jax.random.normal(ks[0], (BATCH, SEQ, D_MODEL), f32),
        'mem': jax.random.normal(ks[1], (BATCH, N_MEM, D_MODEL), f32),
        'positions': positions,
        'mix_norm_pre': gain(ks[3], (DEPTH, D_MODEL)),
        'w_in': dense(ks[4], (DEPTH, D_MODEL, IN_WIDTH), D_MODEL),
        'cv_w': dense(ks[5], (DEPTH, CV_KERNEL, CV_WIDTH), CV_KERNEL),
        'cv_b': bias(ks[6], (DEPTH, CV_WIDTH)),
        'cv_ln_g': gain(ks[7], (DEPTH, CV_WIDTH)),
        'cv_ln_b': bias(ks[8], (DEPTH, CV_WIDTH)),
        'cv_pw_w': dense(ks[9], (DEPTH, CV_WIDTH, CV_WIDTH), CV_WIDTH),
        'cv_pw_b': bias(ks[10], (DEPTH, CV_WIDTH)),
        'w_out': dense(ks[11], (DEPTH, MIX_WIDTH, D_MODEL), MIX_WIDTH),
        'mix_norm_post': gain(ks[12], (DEPTH, D_MODEL)),
        'x_norm_pre': gain(ks[13], (DEPTH, D_MODEL)),
        'mem_norm': gain(ks[14], (DEPTH, D_MODEL)),
        'x_wq': dense(ks[15], (DEPTH, D_MODEL, D_MODEL), D_MODEL),
        'x_wk': dense(ks[16], (DEPTH, D_MODEL, D_MODEL), D_MODEL),
        'x_wv': dense(ks[17], (DEPTH, D_MODEL, D_MODEL), D_MODEL),
        'x_wo': dense(ks[18], (DEPTH, D_MODEL, D_MODEL), D_MODEL),
        'x_norm_post': gain(ks[19], (DEPTH, D_MODEL)),
        'ffn_norm_pre': gain(ks[20], (DEPTH, D_MODEL)),
        'ffn_w_up': dense(ks[21], (DEPTH, D_MODEL, 2 * D_FF), D_MODEL),
        'ffn_conv_w': dense(ks[22], (DEPTH, FFN_KERNEL, 2 * D_FF), FFN_KERNEL),
        'ffn_conv_b': bias(ks[23], (DEPTH, 2 * D_FF)),
        'ffn_w_down': dense(ks[24], (DEPTH, D_FF, D_MODEL), D_FF),
        'ffn_norm_post': gain(ks[25], (DEPTH, D_MODEL)),
    }

def reference(x, mem, positions, mix_norm_pre, w_in, cv_w, cv_b, cv_ln_g, cv_ln_b, cv_pw_w, cv_pw_b,
              w_out, mix_norm_post, x_norm_pre, mem_norm, x_wq, x_wk, x_wv, x_wo, x_norm_post,
              ffn_norm_pre, ffn_w_up, ffn_conv_w, ffn_conv_b, ffn_w_down, ffn_norm_post):
    h = x
    for l in range(DEPTH):
        y = hybrid_mixer(rms_norm(h, mix_norm_pre[l]), positions, w_in[l], cv_w[l], cv_b[l],
                         cv_ln_g[l], cv_ln_b[l], cv_pw_w[l], cv_pw_b[l], w_out[l])
        h = h + rms_norm(y, mix_norm_post[l])
        y = memory_cross_attention(rms_norm(h, x_norm_pre[l]), rms_norm(mem, mem_norm[l]),
                                   x_wq[l], x_wk[l], x_wv[l], x_wo[l])
        h = h + rms_norm(y, x_norm_post[l])
        y = conv_ffn(rms_norm(h, ffn_norm_pre[l]), ffn_w_up[l], ffn_conv_w[l], ffn_conv_b[l], ffn_w_down[l])
        h = h + rms_norm(y, ffn_norm_post[l])
    return h


_drawn_inputs = setup_inputs


def setup_inputs(seed=0):
    import zlib

    import numpy as np

    out = dict(_drawn_inputs(seed))
    spreads = {}
    factors = {'cv_ln_g': 3.689,
     'cv_ln_b': 4.655,
     'mix_norm_post': 2.884,
     'x_norm_pre': 3.329,
     'x_norm_post': 3.29,
     'ffn_norm_pre': 2.988,
     'ffn_conv_b': 2.858,
     'ffn_norm_post': 4.114,
     'cv_pw_b': 2.975}
    for name, (base, spread) in spreads.items():
        noise = np.random.default_rng([zlib.crc32(name.encode()), seed]).standard_normal(out[name].shape)
        drawn = base * np.exp(spread * noise) if base else spread * noise
        out[name] = jnp.asarray(drawn.astype(out[name].dtype))
    for name, factor in factors.items():
        out[name] = (out[name] * factor).astype(out[name].dtype)
    return out
```

```python
from contextlib import ExitStack

import numpy as np

import concourse.bass as bass
from concourse import mybir

F32 = mybir.dt.float32
F32R = mybir.dt.float32r
BF16 = mybir.dt.bfloat16
I32 = mybir.dt.int32
ACT = mybir.ActivationFunctionType
ALU = mybir.AluOpType
AX_X = mybir.AxisListType.X

P = 128
DEPTH = 2
D = 1024
SEQ = 256
TOK = SEQ // P
KC = D // P
HD = 64
SB_W, CV_W, DL_W = 256, 256, 512
DL_HEADS = DL_W // HD
CV_K = 31
D_FF = 2816
FFC = D_FF // P
X_HEADS = 4
EPS = 1e-6
NT = 512
HALF = HD // 2

UNITS = 2
GW = UNITS * NT
PER_TILE = KC // UNITS
UP_TILES = 2 * D_FF // NT
DOWN_GROUPS = FFC // UNITS
G_WK0 = 0
G_IN = G_WK0 + PER_TILE
G_CV, G_DLQ, G_DLK, G_DLV, G_SBQK, G_SBV = (G_IN + i * PER_TILE for i in range(6))
G_WK1 = G_SBV + PER_TILE // 2
G_WV0 = G_WK1 + PER_TILE
G_OUT = G_WV0 + PER_TILE
G_WV1 = G_OUT + 2 * PER_TILE
G_XQ = G_WV1 + PER_TILE
G_XO = G_XQ + 2 * PER_TILE
G_UP = G_XO + 2 * PER_TILE
G_DOWN = G_UP + UP_TILES * PER_TILE
GROUPS = G_DOWN + 2 * DOWN_GROUPS
RING = 4
AHEAD = RING - 1

MIX_ORDER = (4, 5, 6, 7, 0, 2, 3, 1)

PC_CVW = 0
PC_CVB = PC_CVW + 2 * CV_K
PC_LNG = PC_CVB + 2
PC_LNB = PC_LNG + 2
PC_PWB = PC_LNB + 2
PC_FW = PC_PWB + 2
PC_FB = PC_FW + 3 * 2 * FFC
PC = PC_FB + 2 * FFC

AW = 3 * P
CC_ID = 0
CC_TRI = CC_ID + P
CC_ONE = CC_TRI + P
CC_SB = CC_ONE + P
CC_NEG = CC_SB + 2 * AW
CC_MUL = CC_NEG + AW
CC_FRQ = CC_MUL + AW
CC = CC_FRQ + HALF

MEM_G, MIX_PRE, MIX_POST, X_PRE, X_POST, FFN_PRE, FFN_POST = range(7)


class Chain:

    def __init__(self, engine, sem):
        self.engine, self.sem, self.n = engine, sem, 0

    def link(self, instruction):
        self.n += 1
        instruction.then_inc(self.sem, 1)
        self.engine.wait_ge(self.sem, self.n)

    def clear(self):
        if self.n:
            self.engine.sem_clear(self.sem)
        self.n = 0


class Signal:

    def __init__(self, sem, per_layer, before=0, unit=1):
        self.sem, self.per_layer, self.before, self.unit = sem, per_layer, before, unit


    def at(self, layer, n):
        return (layer * self.per_layer + (self.before + n)) * self.unit


def hybrid_trunk(nc, x, mem, pos, consts, gains, params, pw, stream, out):
    with ExitStack() as ctx:
        def sb(name, cols, dt=F32):
            return ctx.enter_context(nc.sbuf_tensor(name, [P, cols], dt))

        def signal(name, per_layer, before=0, unit=1):
            return Signal(ctx.enter_context(nc.semaphore(name)), per_layer, before, unit)

        raw = sb("raw", RING * GW)
        whi = sb("whi", RING * GW, F32R)
        wlo = sb("wlo", RING * GW, F32R)
        h = sb("h", TOK * D)
        xn = sb("xn", TOK * D)
        xT_hi = sb("xT_hi", KC * SEQ, F32R)
        xT_lo = sb("xT_lo", KC * SEQ, F32R)
        oT_hi = sb("oT_hi", KC * SEQ, F32R)
        oT_lo = sb("oT_lo", KC * SEQ, F32R)
        mT_hi = sb("mT_hi", KC * SEQ, F32R)
        mT_lo = sb("mT_lo", KC * SEQ, F32R)
        memn = sb("memn", TOK * D)
        KT = sb("KT", KC * SEQ)
        V = sb("V", TOK * D)
        gpre = sb("gpre", D)
        gpost = sb("gpost", D)
        par = sb("par", PC)
        pww = sb("pww", 2 * CV_W)
        cst = sb("cst", CC)
        trig = sb("trig", TOK * 2 * HALF)
        stat = sb("stat", 96)
        posi = sb("posi", TOK, I32)
        junk = sb("junk", TOK * D, BF16)
        g_bytes = FFC * SEQ * 4
        ARENA = 48 * 1024 // 4
        base = nc.sbuf_base
        arena = sb("arena", ARENA)
        gT_hi = nc.alloc_sbuf_tensor_at("gT_hi", [P, FFC * SEQ], F32R, offset=base)
        gT_lo = nc.alloc_sbuf_tensor_at("gT_lo", [P, FFC * SEQ], F32R, offset=base + g_bytes)
        assert 2 * g_bytes <= ARENA * 4

        taken = [0]

        def part(cols):
            taken[0] += cols
            assert taken[0] <= ARENA, taken[0] - ARENA
            return arena[:, taken[0] - cols:taken[0]]

        glu = part(TOK * CV_W)
        gpad = part(2 * (CV_K - 1 + SEQ)).rearrange("p (c n) -> p c n", c=2)
        cacc = part(2 * SEQ)
        lnn = part(TOK * CV_W)
        sil = sig = part(2 * SEQ)
        sb_a = part(4 * 2 * AW)
        zs, sp, tt = (sb_a[:, i * 2 * AW:(i + 1) * 2 * AW] for i in range(3))
        qr, kr = sb_a[:, 0:TOK * NT], sb_a[:, TOK * NT:2 * TOK * NT]
        ra, rb = sb_a[:, 2 * TOK * NT:2 * TOK * NT + NT], sb_a[:, 2 * TOK * NT + NT:2 * TOK * NT + 2 * NT]
        dqT = part(4 * SEQ).rearrange("p (c n) -> p c n", c=4)
        dkT = part(4 * SEQ).rearrange("p (c n) -> p c n", c=4)
        dlv = part(TOK * NT)
        sbT = part(4 * SEQ).rearrange("p (c n) -> p c n", c=4)
        sbv = part(TOK * SB_W)
        sm0 = part(2 * AW)
        sms = [[sm0[:, 0:AW], sm0[:, AW:2 * AW]], [V[:, NT:NT + AW], V[:, D + NT:D + NT + AW]]]
        pT = part(2 * AW).rearrange("p (h n) -> p h n", h=2)
        sb_w = [a.rearrange("p c n -> p (c n)")[:, 0:2 * AW] for a in (dqT, dkT)]
        ktok = xn[:, 0:TOK * NT]
        sbst = xn[:, TOK * NT:2 * TOK * NT]
        taken[0] = 0
        qT = part(KC * SEQ).rearrange("p (c n) -> p c n", c=KC)
        xp = part(2 * TOK * SEQ).rearrange("p (b t n) -> p b t n", b=2, t=TOK)
        xpT = part(2 * SEQ)
        ffy = [KT[:, b * 4 * SEQ:(b + 1) * 4 * SEQ].rearrange("p (c n) -> p c n", c=4) for b in range(2)]
        ffg = [V[:, b * 2 * SEQ:(b + 1) * 2 * SEQ] for b in range(2)]
        ust = [xn[:, b * TOK * NT:(b + 1) * TOK * NT] for b in range(2)]

        def bank(name):
            return ctx.enter_context(nc.psum_tensor(name, [P, NT], F32))

        accs = [[bank(f"acc{s}{t}") for t in range(TOK)] for s in range(2)]
        psA = ctx.enter_context(nc.psum_tensor("psAB", [P, 2, NT], F32))
        psAB = [psA[:, 0], psA[:, 1]]
        psC = ctx.enter_context(nc.psum_tensor("psCD", [P, 2, NT], F32))
        psCD = [psC[:, 0], psC[:, 1]]

        attended = accs[1][1][:, 0:SEQ]

        ident = cst[:, CC_ID:CC_ID + P]
        tri = cst[:, CC_TRI:CC_TRI + P]
        ones = cst[:, CC_ONE:CC_ONE + P]
        sbmask = cst[:, CC_SB:CC_SB + 2 * AW]
        negm = cst[:, CC_NEG:CC_NEG + AW]
        mult = cst[:, CC_MUL:CC_MUL + AW]

        raw_in = [signal(f"raw_in{s}", GROUPS // RING, unit=16) for s in range(RING)]
        w_hi = signal("w_hi", GROUPS)
        w_lo = signal("w_lo", GROUPS)
        w_used = signal("w_used", GROUPS, before=RING)
        mem_in = signal("mem_in", 0, before=1, unit=16)
        cst_in = signal("cst_in", 0, before=1, unit=16)
        x_in = signal("x_in", 0, before=1, unit=16)
        pos_in = signal("pos_in", 0, before=1, unit=16)
        trig_arg = signal("trig_arg", 0, before=1)
        trig_ready = signal("trig_ready", 0, before=1)
        mgain_in = signal("mgain_in", 0, before=1, unit=16)
        gpre_in = signal("gpre_in", 4, before=1, unit=16)
        gpost_in = signal("gpost_in", 3, before=1, unit=16)
        par_in = signal("par_in", 2, before=2, unit=16)
        mem_sq = signal("mem_sq", 0, before=TOK)
        mem_ms = signal("mem_ms", 0, before=TOK)
        mem_rs = signal("mem_rs", 0, before=TOK)
        mg_done = signal("mg_done", TOK, before=TOK)
        mt_tr = signal("mt_tr", 2 * TOK, before=2 * TOK)
        mt_hi = signal("mt_hi", 2 * TOK, before=2 * TOK)
        mt_lo = signal("mt_lo", 2 * TOK, before=2 * TOK)
        h_ready = signal("h_ready", 3 * 2 * TOK, before=2 * TOK)
        h_sq = signal("h_sq", 3 * 2 * TOK)
        h_ms = signal("h_ms", 3 * TOK)
        h_rs = signal("h_rs", 3 * TOK)
        xn_ready = signal("xn_ready", 3 * 2 * TOK)
        xt_tr = signal("xt_tr", 3 * 2 * TOK)
        xt_hi = signal("xt_hi", 3 * 2 * TOK)
        xt_lo = signal("xt_lo", 3 * 2 * TOK)
        y_tile0 = signal("y_tile0", 4)
        y_sq = signal("y_sq", 3 * 2 * TOK)
        y_ms = signal("y_ms", 3 * TOK)
        y_rs = signal("y_rs", 3 * TOK)
        k_in = signal("k_in", 2 * TOK)
        k_tr = signal("k_tr", 2 * TOK)
        KT_in = signal("KT_in", 2 * TOK)
        V_in = signal("V_in", 2 * TOK)
        cv_sig = signal("cv_sig", TOK)
        cv_g = signal("cv_g", TOK)
        g_tr = signal("g_tr", TOK)
        gpad_zero = signal("gpad_zero", 1)
        gpad_in = signal("gpad_in", TOK)
        tap0 = signal("tap0", 2)
        conv_done = signal("conv_done", 2)
        ln_tr = signal("ln_tr", TOK)
        ln_ms = signal("ln_ms", TOK)
        ln_rs = signal("ln_rs", TOK)
        ln_n = signal("ln_n", TOK)
        ln_tb = signal("ln_tb", 2)
        silu = signal("silu", 2)
        pw_done = signal("pw_done", 2)
        q_roped = signal("q_roped", TOK)
        k_roped = signal("k_roped", TOK)
        q_tr = signal("q_tr", TOK)
        kr_tr = signal("kr_tr", TOK)
        dqT_in = signal("dqT_in", TOK)
        dkT_in = signal("dkT_in", TOK)
        dlv_in = signal("dlv_in", TOK)
        sbst_in = signal("sbst_in", TOK)
        sb_tr = signal("sb_tr", TOK)
        sbT_in = signal("sbT_in", TOK)
        sbv_in = signal("sbv_in", 1)
        s_done = signal("s_done", DL_HEADS)
        nb_ready = signal("nb_ready", DL_HEADS)
        exp_done = signal("exp_done", DL_HEADS)
        den_ready = signal("den_ready", DL_HEADS)
        p_ready = signal("p_ready", DL_HEADS)
        p_tr = signal("p_tr", DL_HEADS)
        pT_in = signal("pT_in", DL_HEADS)
        o_done = signal("o_done", DL_HEADS // 2)
        z_done = signal("z_done", 2)
        zs_ready = signal("zs_ready", 2)
        sp0_ready = signal("sp0_ready", 2)
        sp_ready = signal("sp_ready", 2)
        b_done = signal("b_done", 2)
        t_ready = signal("t_ready", 2)
        a_ready = signal("a_ready", 2)
        sbo_done = signal("sbo_done", 2)
        mix_hi = signal("mix_hi", KC)
        mix_lo = signal("mix_lo", KC)
        qx_in = signal("qx_in", 2 * TOK)
        qx_tr = signal("qx_tr", 2 * TOK)
        qT_in = signal("qT_in", 2 * TOK)
        xs_done = signal("xs_done", X_HEADS)
        xnb = signal("xnb", X_HEADS)
        xe_done = signal("xe_done", X_HEADS)
        xp_ready = signal("xp_ready", X_HEADS)
        xp_tr = signal("xp_tr", X_HEADS)
        xpT_in = signal("xpT_in", X_HEADS)
        xo_done = signal("xo_done", X_HEADS)
        xo_hi = signal("xo_hi", X_HEADS)
        xo_lo = signal("xo_lo", X_HEADS)
        u_in = signal("u_in", TOK * UP_TILES)
        u_tr = signal("u_tr", 2 * UP_TILES)
        y_tap2 = signal("y_tap2", UP_TILES)
        y_conv = signal("y_conv", UP_TILES)
        gelu_done = signal("gelu_done", UP_TILES)
        gv_done = signal("gv_done", UP_TILES)
        g_hi = signal("g_hi", UP_TILES)
        g_lo = signal("g_lo", UP_TILES)
        half_set = signal("half_set", 0, before=1)
        dve_chain = ctx.enter_context(nc.semaphore("dve_chain"))
        act_chain = ctx.enter_context(nc.semaphore("act_chain"))
        out_done = signal("out_done", 0, before=TOK, unit=16)

        def st(i, n=1):
            return stat[:, i:i + n]

        S_HSQ, S_HMS, S_HRS, S_H0, S_YSQ, S_YMS, S_YRS, S_Y0, S_POW = 0, 4, 6, 8, 10, 14, 16, 18, 20
        S_MX, S_NB, S_DEN, S_RDEN = 24, 32, 40, 48
        S_BN, S_MV, S_LMS, S_LRS = 56, 68, 72, 74
        S_XMX, S_XNB, S_XDEN, S_XRD = 76, 80, 84, 88

        def chunks(buf, b, t):
            return buf[:, :].rearrange("p (c n) -> p c n", c=KC)[:, 4 * b:4 * b + 4, t * P:(t + 1) * P]

        def blocks(ps, n=4):
            return ps[:, 0:n * P].rearrange("p (c n) -> p c n", c=n)

        block = ctx.enter_context(nc.Block())


        @block.sync
        def _(sp_):
            tiles = lambda a: a.rearrange("(t p) n -> p t n", p=P)
            sp_.dma_start(memn[:, :].rearrange("p (t n) -> p t n", t=TOK), tiles(mem)).then_inc(mem_in.sem, 16)
            sp_.dma_start(gpre[:, :], gains[0, MEM_G, :].partition_broadcast(P)).then_inc(mgain_in.sem, 16)
            sp_.dma_start(cst[:, :], consts).then_inc(cst_in.sem, 16)
            for s in range(2):
                sp_.dma_start(raw[:, s * GW:(s + 1) * GW], stream[s]).then_inc(raw_in[s].sem, 16)
            sp_.dma_start(h[:, :].rearrange("p (t n) -> p t n", t=TOK), tiles(x)).then_inc(x_in.sem, 16)
            for s in range(2, RING):
                sp_.dma_start(raw[:, s * GW:(s + 1) * GW], stream[s]).then_inc(raw_in[s].sem, 16)
            with sp_.Fori(1, DEPTH * GROUPS // RING) as r:
                for s in range(RING):
                    sp_.wait_ge(w_lo.sem, r * RING + (s + 1 - RING))
                    sp_.dma_start(raw[:, s * GW:(s + 1) * GW], stream[r * RING + s]).then_inc(raw_in[s].sem, 16)
            for s in range(RING):
                sp_.wait_ge(w_lo.sem, DEPTH * GROUPS + s + 1 - RING)
                sp_.dma_start(raw[:, s * GW:(s + 1) * GW], stream[s]).then_inc(raw_in[s].sem, 16)
            for t in range(TOK):
                sp_.wait_ge(h_ready.sem, h_ready.at(DEPTH, 2 * (t + 1) - 2 * TOK))
                sp_.dma_start(out[t * P:(t + 1) * P, :], h[:, t * D:(t + 1) * D]).then_inc(out_done.sem, 16)
            for s in range(RING):
                sp_.wait_ge(raw_in[s].sem, raw_in[s].at(DEPTH, 1))
            sp_.wait_ge(out_done.sem, out_done.at(0, 0))

        @block.gpsimd
        def _(pool):
            def gain(buf, landed, layer, row):
                pool.dma_start(buf[:, :], gains[layer, row, :].partition_broadcast(P)).then_inc(landed.sem, 16)

            def load_params(layer):
                pool.dma_start(par[:, :], params[layer]).then_inc(par_in.sem, 16)
                pool.dma_start(pww[:, :], pw[layer]).then_inc(par_in.sem, 16)

            def rsqrt(col_out, col_in):
                return pool.tensor_tensor(st(col_out), st(col_in), st(S_POW), ALU.pow)

            pool.dma_start(posi[:, :], pos).then_inc(pos_in.sem, 16)
            pool.memset(st(S_POW), -0.5).then_inc(half_set.sem, 1)
            gain(gpost, gpost_in, 0, MIX_POST)
            load_params(0)
            pool.wait_ge(half_set.sem, 1)
            for t in range(TOK):
                pool.wait_ge(mem_ms.sem, mem_ms.at(0, t - TOK + 1))
                rsqrt(S_HRS + t, S_HMS + t).then_inc(mem_rs.sem, 1)
            pool.wait_ge(mg_done.sem, mg_done.at(0, 0))
            gain(gpre, gpre_in, 0, MIX_PRE)

            def before_sub_layer(l, i, t):
                pool.wait_ge(h_ms.sem, h_ms.at(l, TOK * i + t + 1))
                rsqrt(S_HRS + t, S_HMS + t).then_inc(h_rs.sem, 1)

            for t in range(TOK):
                before_sub_layer(0, 0, t)

            with pool.Fori(0, DEPTH) as l:
                def turn(i):
                    for t in range(TOK):
                        pool.wait_ge(y_ms.sem, y_ms.at(l, TOK * i + t + 1))
                        rsqrt(S_YRS + t, S_YMS + t).then_inc(y_rs.sem, 1)
                        before_sub_layer(l, i + 1, t)

                pool.wait_ge(xn_ready.sem, xn_ready.at(l, 2 * TOK))
                gain(gpre, gpre_in, l, X_PRE)
                for t in range(TOK):
                    pool.wait_ge(ln_ms.sem, ln_ms.at(l, t + 1))
                    rsqrt(S_LRS + t, S_LMS + t).then_inc(ln_rs.sem, 1)
                turn(0)
                pool.wait_ge(h_ready.sem, h_ready.at(l, 2 * TOK))
                gain(gpost, gpost_in, l, X_POST)
                pool.wait_ge(xn_ready.sem, xn_ready.at(l, 4 * TOK))
                gain(gpre, gpre_in, l, FFN_PRE)
                turn(1)
                pool.wait_ge(h_ready.sem, h_ready.at(l, 4 * TOK))
                gain(gpost, gpost_in, l, FFN_POST)
                pool.wait_ge(xn_ready.sem, xn_ready.at(l, 6 * TOK))
                gain(gpre, gpre_in, l + 1, MEM_G)
                pool.wait_ge(mg_done.sem, mg_done.at(l, TOK))
                gain(gpre, gpre_in, l + 1, MIX_PRE)
                turn(2)
                pool.wait_ge(h_ready.sem, h_ready.at(l, 6 * TOK))
                gain(gpost, gpost_in, l + 1, MIX_POST)
                load_params(l + 1)
            pool.wait_ge(gpre_in.sem, gpre_in.at(DEPTH, 0))
            pool.wait_ge(gpost_in.sem, gpost_in.at(DEPTH, 0))
            pool.wait_ge(par_in.sem, par_in.at(DEPTH, 0))

        @block.scalar
        def _(act):
            own = Chain(act, act_chain)
            def memory_hi(l, t, n0=0):
                for b in range(2):
                    act.wait_ge(mt_tr.sem, mt_tr.at(l, n0 + 2 * t + b + 1))
                    act.activation(chunks(mT_hi, b, t), blocks(psCD[b]), ACT.Copy).then_inc(mt_hi.sem, 1)

            def split_group(l, g):
                s = g % RING
                act.wait_ge(raw_in[s].sem, raw_in[s].at(l, g // RING + 1))
                act.wait_ge(w_used.sem, w_used.at(l, g + 1 - RING))
                act.activation(whi[:, s * GW:(s + 1) * GW], raw[:, s * GW:(s + 1) * GW], ACT.Copy).then_inc(w_hi.sem, 1)

            def squares_h(l, i, t):
                for n in range(2):
                    cols = slice(t * D + n * NT, t * D + (n + 1) * NT)
                    act.wait_ge(h_ready.sem, h_ready.at(l, 2 * TOK * (i - 1) + 2 * t + n + 1))
                    act.activation(junk[:, cols], h[:, cols], ACT.Square, accum_out=st(S_HSQ + 2 * t + n)).then_inc(h_sq.sem, 1)

            act.wait_ge(mem_in.sem, 16)
            for t in range(TOK):
                act.activation(junk[:, t * D:(t + 1) * D], memn[:, t * D:(t + 1) * D], ACT.Square,
                               accum_out=st(S_HSQ + t)).then_inc(mem_sq.sem, 1)
            split_group(0, 0)
            for t in range(TOK):
                memory_hi(0, t, -2 * TOK)
            for g in range(1, RING):
                split_group(0, g)
            act.wait_ge(trig_arg.sem, 1)
            act.activation(trig[:, :], trig[:, :], ACT.Sin).then_inc(trig_ready.sem, 1)

            act.wait_ge(x_in.sem, 16)
            for t in range(TOK):
                squares_h(0, 0, t)

            with act.Fori(0, DEPTH) as l:
                split_to = [RING]

                def split(upto):
                    for g in range(split_to[0], upto + 1):
                        split_group(l, g)
                    split_to[0] = max(split_to[0], upto + 1)

                def square_y(t, n, bank_set):
                    act.activation(junk[:, t * D + n * NT:t * D + (n + 1) * NT], accs[bank_set][t][:, :],
                                   ACT.Square, accum_out=st(S_YSQ + 2 * t + n)).then_inc(y_sq.sem, 1)

                def squares_first(bank_set, g_end):
                    act.wait_ge(w_used.sem, w_used.at(l, g_end))
                    for t in range(TOK):
                        square_y(t, 0, bank_set)

                def turn(i, halves, g_end):
                    for n, bank_set, ready, _ in halves:
                        act.wait_ge(y_tile0.sem, y_tile0.at(l, ready))
                        square_y(0, n, bank_set)
                    split(g_end + 1)
                    squares_h(l, i + 1, 0)
                    for n, bank_set, _, g in halves:
                        act.wait_ge(w_used.sem, w_used.at(l, g))
                        square_y(1, n, bank_set)
                    if i == 1:
                        input_hi(i + 1, 0)
                        split(g_end + 2)
                    else:
                        split(g_end + 3)
                        if i == 0:
                            input_hi(i + 1, 0)
                    squares_h(l, i + 1, 1)

                def input_hi(i, t):
                    for b in range(2):
                        act.wait_ge(xt_tr.sem, xt_tr.at(l, 2 * TOK * i + 2 * t + b + 1))
                        act.activation(chunks(xT_hi, b, t), blocks(psCD[b]), ACT.Copy).then_inc(xt_hi.sem, 1)

                def k_rows(n, src, g_end):
                    act.wait_ge(w_used.sem, w_used.at(l, g_end))
                    for t in range(TOK):
                        act.activation(ktok[:, t * NT:(t + 1) * NT], src[t], ACT.Copy).then_inc(k_in.sem, 1)

                def k_columns(n):
                    for t in range(TOK):
                        act.wait_ge(k_tr.sem, k_tr.at(l, TOK * n + t + 1))
                        act.activation(chunks(KT, n, t), blocks(psCD[t]), ACT.Copy).then_inc(KT_in.sem, 1)

                def v_rows(n, src, g_end):
                    act.wait_ge(w_used.sem, w_used.at(l, g_end))
                    for t in range(TOK):
                        act.activation(V[:, t * D + n * NT:t * D + (n + 1) * NT], src[t], ACT.Copy).then_inc(V_in.sem, 1)

                def exp_pair(c):
                    for r in range(2):
                        act.wait_ge(nb_ready.sem, nb_ready.at(l, 2 * c + r + 1))
                        for q, (a, b) in enumerate(((0, P), (P, AW))):
                            p = sms[c % 2][r][:, a:b]
                            e = act.activation(p, p, ACT.Exp, bias=st(S_NB + 4 * (c % 2) + 2 * r + q),
                                               scale=HD ** -0.5)
                        e.then_inc(exp_done.sem, 1)

                def scale_pair(c):
                    for r in range(2):
                        act.wait_ge(den_ready.sem, den_ready.at(l, 2 * c + r + 1))
                        for q, (a, b) in enumerate(((0, P), (P, AW))):
                            p = sms[c % 2][r][:, a:b]
                            e = act.activation(p, p, ACT.Copy, scale=st(S_RDEN + 4 * (c % 2) + 2 * r + q))
                        e.then_inc(p_ready.sem, 1)

                def p_columns(c):
                    for r in range(2):
                        act.wait_ge(p_tr.sem, p_tr.at(l, 2 * c + r + 1))
                        if c and not r:
                            act.wait_ge(o_done.sem, o_done.at(l, c))
                        act.activation(pT[:, r, :], psCD[r][:, 0:AW], ACT.Copy).then_inc(pT_in.sem, 1)

                def mixed_hi(chunk, ready, n, src, bias=None):
                    act.wait_ge(ready.sem, ready.at(l, n))
                    act.activation(oT_hi[:, chunk * SEQ:(chunk + 1) * SEQ], src,
                                   ACT.Copy if bias is None else ACT.Identity,
                                   bias=0.0 if bias is None else bias).then_inc(mix_hi.sem, 1)

                def softplus_pair(c):
                    act.wait_ge(zs_ready.sem, zs_ready.at(l, c + 1))
                    if c:
                        act.wait_ge(t_ready.sem, t_ready.at(l, c))
                    own.link(act.activation(sp, zs, ACT.Abs))
                    own.link(act.activation(sp, sp, ACT.Exp, scale=-1.0))
                    act.activation(sp, sp, ACT.Ln, bias=1.0).then_inc(sp0_ready.sem, 1)

                def sb_weights(c):
                    act.wait_ge(t_ready.sem, t_ready.at(l, c + 1))
                    act.activation(sb_w[c], tt, ACT.Exp).then_inc(a_ready.sem, 1)

                input_hi(0, 0)
                split(6)
                k_rows(0, psAB, G_WK0 + PER_TILE)
                split(G_CV + PER_TILE - 1)
                input_hi(0, 1)
                split(G_CV + PER_TILE - 1 + AHEAD)
                act.wait_ge(w_used.sem, w_used.at(l, G_CV + PER_TILE))
                for t in range(TOK):
                    act.activation(sig[:, t * CV_W:(t + 1) * CV_W], accs[0][t][:, CV_W:2 * CV_W], ACT.Sigmoid).then_inc(cv_sig.sem, 1)
                k_columns(0)
                split(G_DLQ + 1 + AHEAD)
                for t in range(TOK):
                    act.wait_ge(g_tr.sem, g_tr.at(l, t + 1))
                    act.activation(gpad[:, :, CV_K - 1 + t * P:CV_K - 1 + (t + 1) * P],
                                   blocks(psCD[t], 2), ACT.Copy).then_inc(gpad_in.sem, 1)
                act.wait_ge(gpad_zero.sem, gpad_zero.at(l, 1))
                act.wait_ge(gpad_in.sem, gpad_in.at(l, TOK))
                for c in range(2):
                    act.activation(cacc[:, c * SEQ:(c + 1) * SEQ], gpad[:, c, 0:SEQ], ACT.Identity,
                                   scale=par[:, PC_CVW + c * CV_K:PC_CVW + c * CV_K + 1],
                                   bias=par[:, PC_CVB + c:PC_CVB + c + 1]).then_inc(tap0.sem, 1)

                def columns(dst, ready, arrived):
                    for t in range(TOK):
                        act.wait_ge(ready.sem, ready.at(l, t + 1))
                        act.activation(dst[:, :, t * P:(t + 1) * P], blocks(psCD[t]), ACT.Copy).then_inc(arrived.sem, 1)

                split(G_DLK + 1 + AHEAD)
                columns(dqT, q_tr, dqT_in)
                split(G_DLV + 1 + AHEAD)
                columns(dkT, kr_tr, dkT_in)
                split(G_DLV + 3 + AHEAD)
                act.wait_ge(w_used.sem, w_used.at(l, G_DLV + PER_TILE))
                for t in range(TOK):
                    act.activation(dlv[:, t * NT:(t + 1) * NT], accs[1][t][:, :], ACT.Copy).then_inc(dlv_in.sem, 1)
                exp_pair(0)
                split(G_SBQK + AHEAD)
                scale_pair(0)
                exp_pair(1)
                split(G_SBQK + 1 + AHEAD)
                p_columns(0)
                scale_pair(1)
                exp_pair(2)
                split(G_SBQK + 2 + AHEAD)
                mixed_hi(4, o_done, 1, attended)
                p_columns(1)
                scale_pair(2)
                exp_pair(3)
                split(G_SBQK + 3 + AHEAD)
                mixed_hi(5, o_done, 2, attended)
                p_columns(2)
                act.wait_ge(w_used.sem, w_used.at(l, G_SBQK + PER_TILE))
                for t in range(TOK):
                    act.activation(sbst[:, t * NT:(t + 1) * NT], accs[0][t][:, :], ACT.Copy).then_inc(sbst_in.sem, 1)
                scale_pair(3)
                split(G_SBV + AHEAD)
                mixed_hi(6, o_done, 3, attended)
                columns(sbT, sb_tr, sbT_in)
                split(G_SBV + 1 + AHEAD)
                act.wait_ge(w_used.sem, w_used.at(l, G_SBV + PER_TILE // 2))
                act.activation(sbv, accs[1][0][:, :], ACT.Copy).then_inc(sbv_in.sem, 1)
                split(G_WK1 + AHEAD)
                p_columns(3)
                softplus_pair(0)
                mixed_hi(7, o_done, 4, attended)
                split(G_WK1 + 2 + AHEAD)
                sb_weights(0)
                softplus_pair(1)
                split(G_WK1 + 3 + AHEAD)
                k_rows(1, [accs[0][t][:, :] for t in range(TOK)], G_WK1 + PER_TILE)
                split(G_WV0 + AHEAD)
                mixed_hi(0, sbo_done, 1, accs[0][0][:, 0:SEQ])
                split(G_WV0 + 2 + AHEAD)
                sb_weights(1)
                for c in range(2):
                    act.wait_ge(ln_tb.sem, ln_tb.at(l, c + 1))
                    act.activation(sil[:, c * SEQ:(c + 1) * SEQ], psCD[c][:, 0:SEQ], ACT.Silu,
                                   scale=par[:, PC_LNG + c:PC_LNG + c + 1],
                                   bias=par[:, PC_LNB + c:PC_LNB + c + 1]).then_inc(silu.sem, 1)
                split(G_WV0 + 3 + AHEAD)
                for c in range(2):
                    mixed_hi(2 + c, pw_done, c + 1, psCD[c][:, 0:SEQ], par[:, PC_PWB + c:PC_PWB + c + 1])
                v_rows(0, [accs[1][t][:, :] for t in range(TOK)], G_WV0 + PER_TILE)
                split(G_OUT + AHEAD)
                k_columns(1)
                split(G_OUT + 1 + AHEAD)
                mixed_hi(1, sbo_done, 2, psCD[1][:, 0:SEQ])
                split(G_OUT + PER_TILE - 1 + AHEAD)
                squares_first(0, G_OUT + PER_TILE)
                split(G_OUT + 2 * PER_TILE - 1)
                turn(0, [(1, 1, 1, G_OUT + 2 * PER_TILE)], G_OUT + 2 * PER_TILE)

                split(G_WV1 + 3 + AHEAD)
                v_rows(1, psAB, G_WV1 + PER_TILE)
                split(G_XQ + PER_TILE - 1)
                input_hi(1, 1)

                def q_rows(n):
                    act.wait_ge(w_used.sem, w_used.at(l, G_XQ + (n + 1) * PER_TILE))
                    for t in range(TOK):
                        act.activation(xn[:, n * TOK * NT + t * NT:n * TOK * NT + (t + 1) * NT],
                                       accs[n][t][:, :], ACT.Copy).then_inc(qx_in.sem, 1)

                def q_columns(n):
                    for t in range(TOK):
                        act.wait_ge(qx_tr.sem, qx_tr.at(l, TOK * n + t + 1))
                        act.activation(qT[:, 4 * n:4 * n + 4, t * P:(t + 1) * P], blocks(psCD[t]), ACT.Copy).then_inc(qT_in.sem, 1)

                def exp_head(hd):
                    act.wait_ge(xnb.sem, xnb.at(l, hd + 1))
                    if hd >= 2:
                        act.wait_ge(xp_tr.sem, xp_tr.at(l, hd - 1))
                    for t in range(TOK):
                        e = act.activation(xp[:, hd % 2, t, :], psAB[hd % 2][:, t * SEQ:(t + 1) * SEQ], ACT.Exp,
                                           bias=st(S_XNB + 2 * (hd % 2) + t), scale=(D // X_HEADS) ** -0.5,
                                           accum_out=st(S_XDEN + 2 * (hd % 2) + t))
                    e.then_inc(xe_done.sem, 1)

                def xp_columns(hd):
                    act.wait_ge(xp_tr.sem, xp_tr.at(l, hd + 1))
                    if hd:
                        act.wait_ge(xo_done.sem, xo_done.at(l, hd))
                    act.activation(xpT, psCD[0][:, :], ACT.Copy).then_inc(xpT_in.sem, 1)

                def crossed_hi(hd):
                    act.wait_ge(xo_done.sem, xo_done.at(l, hd + 1))
                    act.activation(oT_hi[:, hd * 2 * SEQ:(hd + 1) * 2 * SEQ], psCD[1][:, :], ACT.Copy).then_inc(xo_hi.sem, 1)

                split(G_XQ + PER_TILE - 1 + AHEAD)
                q_rows(0)
                split(G_XQ + PER_TILE + 1 + AHEAD)
                q_columns(0)
                split(G_XQ + PER_TILE + 2 + AHEAD)
                exp_head(0)
                exp_head(1)
                split(G_XQ + 2 * PER_TILE - 1 + AHEAD)
                q_rows(1)
                q_columns(1)
                xp_columns(0)
                exp_head(2)
                crossed_hi(0)
                xp_columns(1)
                exp_head(3)
                split(G_XO + AHEAD)
                crossed_hi(1)
                xp_columns(2)
                split(G_XO + 2 + AHEAD)
                crossed_hi(2)
                xp_columns(3)
                split(G_XO + 4 + AHEAD)
                crossed_hi(3)
                turn(1, [(0, 0, 2, G_XO + 2 * PER_TILE - 2), (1, 1, 3, G_XO + 2 * PER_TILE)], G_XO + 2 * PER_TILE)
                split(G_UP + PER_TILE - 1)
                input_hi(2, 1)

                def up_rows(j):
                    act.wait_ge(w_used.sem, w_used.at(l, G_UP + (j + 1) * PER_TILE))
                    if j >= 2:
                        act.wait_ge(u_tr.sem, u_tr.at(l, 2 * (j - 1)))
                    for t in range(TOK):
                        act.activation(ust[j % 2][:, t * NT:(t + 1) * NT], accs[j % 2][t][:, :], ACT.Copy).then_inc(u_in.sem, 1)

                def gate(j):
                    y = ffy[j % 2]
                    act.wait_ge(u_tr.sem, u_tr.at(l, 2 * (j + 1)))
                    if j >= 2:
                        act.wait_ge(gv_done.sem, gv_done.at(l, j - 1))
                    for c in range(4):
                        fc = (FFC if c >= 2 else 0) + 2 * j + c % 2
                        e = act.activation(y[:, c, :], psCD[c // 2][:, c % 2 * SEQ:(c % 2 + 1) * SEQ], ACT.Identity,
                                           scale=par[:, PC_FW + 3 * fc + 2:PC_FW + 3 * fc + 3],
                                           bias=par[:, PC_FB + fc:PC_FB + fc + 1])
                    e.then_inc(y_tap2.sem, 1)

                def gate_gelu(j):
                    act.wait_ge(y_conv.sem, y_conv.at(l, j + 1))
                    if j >= 2:
                        act.wait_ge(g_lo.sem, g_lo.at(l, j - 1))
                    act.activation(ffg[j % 2].rearrange("p (c n) -> p c n", c=2), ffy[j % 2][:, 0:2, :],
                                   ACT.Gelu_apprx_tanh).then_inc(gelu_done.sem, 1)
                    act.wait_ge(gv_done.sem, gv_done.at(l, j + 1))
                    act.activation(gT_hi[:, 2 * j * SEQ:2 * (j + 1) * SEQ], ffg[j % 2], ACT.Copy).then_inc(g_hi.sem, 1)

                for j in range(UP_TILES):
                    split(G_UP + (j + 1) * PER_TILE - 1 + AHEAD)
                    up_rows(j)
                    split(G_UP + (j + 1) * PER_TILE + 1 + AHEAD)
                    gate(j)
                    split(G_UP + (j + 1) * PER_TILE + 2 + AHEAD)
                    gate_gelu(j)
                split(G_DOWN + 7 + AHEAD)
                memory_hi(l, 0)
                split(G_DOWN + 9 + AHEAD)
                memory_hi(l, 1)
                split(G_DOWN + DOWN_GROUPS - 1 + AHEAD)
                squares_first(1, G_DOWN + DOWN_GROUPS)
                split(GROUPS - 1)
                turn(2, [(1, 0, 4, GROUPS)], GROUPS)
                own.clear()

        @block.vector
        def _(dve):
            own = Chain(dve, dve_chain)
            dve.wait_ge(mem_in.sem, 16)
            tiny = lambda c: st(c, TOK)

            def split_group(l, g):
                s = g % RING
                cols = slice(s * GW, (s + 1) * GW)
                dve.wait_ge(w_hi.sem, w_hi.at(l, g + 1))
                dve.tensor_tensor(wlo[:, cols], raw[:, cols], whi[:, cols].bitcast(F32), ALU.subtract).then_inc(w_lo.sem, 1)

            def mean_square(out_col, sq_col):
                return dve.tensor_scalar(st(out_col), st(sq_col), 1.0 / D, EPS, ALU.mult, ALU.add)

            for t in range(TOK):
                dve.wait_ge(mem_sq.sem, mem_sq.at(0, t - TOK + 1))
                mean_square(S_HMS + t, S_HSQ + t).then_inc(mem_ms.sem, 1)
            for t in range(TOK):
                dve.wait_ge(mem_rs.sem, mem_rs.at(0, t - TOK + 1))
                own.link(dve.tensor_scalar(memn[:, t * D:(t + 1) * D], memn[:, t * D:(t + 1) * D], st(S_HRS + t), None,
                                           ALU.mult))

            def memory_gain():
                for t in range(TOK):
                    dve.tensor_tensor(xn[:, t * D:(t + 1) * D], memn[:, t * D:(t + 1) * D], gpre[:, :],
                                      ALU.mult).then_inc(mg_done.sem, 1)

            def memory_lo(l, t, n0=0):
                for b in range(2):
                    dve.wait_ge(mt_hi.sem, mt_hi.at(l, n0 + 2 * t + b + 1))
                    dve.tensor_tensor(chunks(mT_lo, b, t), blocks(psCD[b]), chunks(mT_hi, b, t).bitcast(F32),
                                      ALU.subtract).then_inc(mt_lo.sem, 1)

            dve.wait_ge(mgain_in.sem, 16)
            memory_gain()
            split_group(0, 0)
            for t in range(TOK):
                memory_lo(0, t, -2 * TOK)
            for g in range(1, RING):
                split_group(0, g)
            scr = arena[:, 0:3 * TOK * 2 * HALF]
            ang, turns_ = scr[:, 0:TOK * 2 * HALF], scr[:, TOK * 2 * HALF:2 * TOK * 2 * HALF]
            posf = scr[:, 2 * TOK * 2 * HALF:2 * TOK * 2 * HALF + TOK]
            dve.wait_ge(pos_in.sem, 16)
            own.link(dve.tensor_copy(posf, posi[:, :]))
            for t in range(TOK):
                for k in range(2):
                    e = dve.tensor_scalar(ang[:, (2 * t + k) * HALF:(2 * t + k + 1) * HALF],
                                          cst[:, CC_FRQ:CC_FRQ + HALF], posf[:, t:t + 1], None, ALU.mult)
            own.link(e)
            for t in range(TOK):
                for k in range(2):
                    cols = slice((2 * t + k) * HALF, (2 * t + k + 1) * HALF)
                    e = dve.tensor_scalar(turns_[:, cols], ang[:, cols], float(1 / (2 * np.pi)), 0.25 if k == 0 else 0.0,
                                          ALU.mult, ALU.add)
            own.link(e)
            nearest = 1.5 * 2.0 ** 23
            own.link(dve.tensor_scalar(turns_, turns_, nearest, -nearest, ALU.add, ALU.add))
            part1 = 6.28125
            part2 = float(np.float32(round((2 * np.pi - part1) * 2 ** 21) / 2 ** 21))
            part3 = float(2 * np.pi - part1 - part2)
            for c in (part1, part2, part3):
                own.link(dve.scalar_tensor_tensor(ang, turns_, -c, ang, ALU.mult, ALU.add))
            for t in range(TOK):
                cols = slice(2 * t * HALF, (2 * t + 1) * HALF)
                e = dve.tensor_scalar(ang[:, cols], ang[:, cols], float(np.pi / 2), None, ALU.add)
            own.link(e)
            pi = 3.1415925
            dve.tensor_scalar(trig[:, :], ang, pi, -pi, ALU.min, ALU.max).then_inc(trig_arg.sem, 1)

            dve.wait_ge(x_in.sem, 16)
            for i in range(2 * TOK):
                dve.memset(st(S_HSQ + i), 0.0).then_inc(h_ready.sem, 1)
            def norm_input(l, i, t):
                dve.wait_ge(h_sq.sem, h_sq.at(l, 2 * TOK * i + 2 * (t + 1)))
                own.link(dve.tensor_scalar(st(S_H0 + t), st(S_HSQ + 2 * t), 1.0 / D, EPS, ALU.mult, ALU.add))
                dve.scalar_tensor_tensor(st(S_HMS + t), st(S_HSQ + 2 * t + 1), 1.0 / D, st(S_H0 + t),
                                         ALU.mult, ALU.add).then_inc(h_ms.sem, 1)

            def norm_scale(l, i, t, n_gain):
                dve.wait_ge(gpre_in.sem, gpre_in.at(l, n_gain))
                dve.wait_ge(h_rs.sem, h_rs.at(l, TOK * i + t + 1))
                for n in range(2):
                    cols = slice(t * D + n * NT, t * D + (n + 1) * NT)
                    dve.scalar_tensor_tensor(xn[:, cols], h[:, cols], st(S_HRS + t),
                                             gpre[:, n * NT:(n + 1) * NT], ALU.mult, ALU.mult).then_inc(xn_ready.sem, 1)

            for t in range(TOK):
                norm_input(0, 0, t)
            for t in range(TOK):
                norm_scale(0, 0, t, 0)
            dve.wait_ge(trig_ready.sem, 1)
            own.clear()

            with dve.Fori(0, DEPTH) as l:
                split_to = [RING]

                def split(upto):
                    for g in range(split_to[0], upto + 1):
                        split_group(l, g)
                    split_to[0] = max(split_to[0], upto + 1)

                def input_lo(i, t):
                    for b in range(2):
                        dve.wait_ge(xt_hi.sem, xt_hi.at(l, 2 * TOK * i + 2 * t + b + 1))
                        dve.tensor_tensor(chunks(xT_lo, b, t), blocks(psCD[b]),
                                          chunks(xT_hi, b, t).bitcast(F32), ALU.subtract).then_inc(xt_lo.sem, 1)

                def output_gain(t, n, bank_set):
                    own.link(dve.tensor_tensor(xn[:, t * D + n * NT:t * D + (n + 1) * NT], accs[bank_set][t][:, :],
                                               gpost[:, n * NT:(n + 1) * NT], ALU.mult))

                def first_half(t):
                    own.link(dve.tensor_scalar(st(S_Y0 + t), st(S_YSQ + 2 * t), 1.0 / D, EPS, ALU.mult, ALU.add))

                def output_first(i, bank_set, g_end, n_gain):
                    dve.wait_ge(w_used.sem, w_used.at(l, g_end))
                    dve.wait_ge(gpost_in.sem, gpost_in.at(l, n_gain))
                    for t in range(TOK):
                        dve.wait_ge(y_sq.sem, y_sq.at(l, 2 * TOK * i + t + 1))
                        output_gain(t, 0, bank_set)
                    for t in range(TOK):
                        first_half(t)

                def turn(i, halves, g_end):
                    for t in range(TOK):
                        for n, bank_set, counts in halves:
                            dve.wait_ge(y_sq.sem, y_sq.at(l, counts[t]))
                            if n:
                                dve.scalar_tensor_tensor(st(S_YMS + t), st(S_YSQ + 2 * t + 1), 1.0 / D,
                                                         st(S_Y0 + t), ALU.mult, ALU.add).then_inc(y_ms.sem, 1)
                            else:
                                first_half(t)
                            output_gain(t, n, bank_set)
                        if not t:
                            split(g_end)
                            add_output(i, t)
                            split(g_end + 1)
                        elif i == 1:
                            input_lo(i + 1, 0)
                            add_output(i, t)
                            split(g_end + 2)
                        else:
                            split(g_end + 2)
                            add_output(i, t)
                            if i == 0:
                                input_lo(i + 1, 0)
                            split(g_end + 3)
                        norm_input(l, i + 1, t)
                        norm_scale(l, i + 1, t, i + 1 if i < 2 else 4)

                def add_output(i, t):
                    dve.wait_ge(y_rs.sem, y_rs.at(l, TOK * i + t + 1))
                    for n in range(2):
                        cols = slice(t * D + n * NT, t * D + (n + 1) * NT)
                        dve.scalar_tensor_tensor(h[:, cols], xn[:, cols], st(S_YRS + t), h[:, cols],
                                                 ALU.mult, ALU.add).then_inc(h_ready.sem, 1)

                def rope(bank_set, dst, g_end, roped):
                    dve.wait_ge(w_used.sem, w_used.at(l, g_end))
                    for t in range(TOK):
                        if t:
                            dve.wait_ge(roped.sem, roped.at(l, t))
                        elif roped is k_roped:
                            dve.wait_ge(q_roped.sem, q_roped.at(l, TOK))
                        x3 = accs[bank_set][t][:, :].rearrange("p (g j) -> p g j", j=HALF)
                        a3 = ra.rearrange("p (g j) -> p g j", j=HALF)
                        b3 = rb.rearrange("p (g j) -> p g j", j=HALF)
                        cs = lambda k: trig[:, (2 * t + k) * HALF:(2 * t + k + 1) * HALF].unsqueeze(1)\
                            .to_broadcast([P, NT // HALF, HALF])
                        dve.tensor_tensor(a3, x3, cs(0), ALU.mult)
                        own.link(dve.tensor_tensor(b3, x3, cs(1), ALU.mult))
                        a4 = ra.rearrange("p (g r j) -> p g r j", r=2, j=HALF)
                        b4 = rb.rearrange("p (g r j) -> p g r j", r=2, j=HALF)
                        d4 = dst[:, t * NT:(t + 1) * NT].rearrange("p (g r j) -> p g r j", r=2, j=HALF)
                        dve.tensor_tensor(d4[:, :, 0], a4[:, :, 0], b4[:, :, 1], ALU.subtract)
                        dve.tensor_tensor(d4[:, :, 1], a4[:, :, 1], b4[:, :, 0], ALU.add).then_inc(roped.sem, 1)

                def scores_max(c):
                    w = 4 * (c % 2)
                    for r in range(2):
                        dve.wait_ge(s_done.sem, s_done.at(l, 2 * c + r + 1))
                        if c >= 2:
                            dve.wait_ge(p_tr.sem, p_tr.at(l, 2 * (c - 2) + r + 1))
                        own.link(dve.memset(st(S_MX + w + 2 * r, 2), -3e38))
                        for q, (a, b) in enumerate(((0, P), (P, AW))):
                            e = dve.tensor_tensor_reduce(sms[c % 2][r][:, a:b], psAB[r][:, a:b], negm[:, a:b], 1.0,
                                                         -3e38, ALU.add, ALU.max, st(S_MX + w + 2 * r + q))
                        own.link(e)
                        dve.tensor_scalar(st(S_NB + w + 2 * r, 2), st(S_MX + w + 2 * r, 2), -HD ** -0.5,
                                          None, ALU.mult).then_inc(nb_ready.sem, 1)

                def probabilities(c):
                    w = 4 * (c % 2)
                    for r in range(2):
                        dve.wait_ge(exp_done.sem, exp_done.at(l, 2 * c + r + 1))
                        for q, (a, b) in enumerate(((0, P), (P, AW))):
                            p = sms[c % 2][r][:, a:b]
                            e = dve.tensor_tensor_reduce(p, p, mult[:, a:b], 1.0, 0.0, ALU.mult, ALU.add,
                                                         st(S_DEN + w + 2 * r + q))
                        own.link(e)
                        dve.reciprocal(st(S_RDEN + w + 2 * r, 2), st(S_DEN + w + 2 * r, 2)).then_inc(den_ready.sem, 1)

                def mixed_lo(n, chunk, src, bias=None):
                    dve.wait_ge(mix_hi.sem, mix_hi.at(l, n))
                    cols = slice(chunk * SEQ, (chunk + 1) * SEQ)
                    if bias is None:
                        e = dve.tensor_tensor(oT_lo[:, cols], src, oT_hi[:, cols].bitcast(F32), ALU.subtract)
                    else:
                        e = dve.scalar_tensor_tensor(oT_lo[:, cols], src, bias, oT_hi[:, cols].bitcast(F32),
                                                     ALU.add, ALU.subtract)
                    e.then_inc(mix_lo.sem, 1)

                def conv_taps(lo, hi):
                    for j in range(lo, hi):
                        for c in range(2):
                            w = par[:, PC_CVW + c * CV_K + j:PC_CVW + c * CV_K + j + 1]
                            src, acc = gpad[:, c, j:j + SEQ], cacc[:, c * SEQ:(c + 1) * SEQ]
                            if j == 1:
                                dve.wait_ge(tap0.sem, tap0.at(l, c + 1))
                            else:
                                dve.wait_ge(own.sem, own.n - (0 if j == CV_K - 1 and c else 1))
                            e = dve.scalar_tensor_tensor(acc, src, w, acc, ALU.mult, ALU.add)
                            if j < CV_K - 1:
                                own.n += 1
                                e.then_inc(own.sem, 1)
                            else:
                                e.then_inc(conv_done.sem, 1)

                def sb_masked(c):
                    dve.wait_ge(z_done.sem, z_done.at(l, c + 1))
                    view = lambda a: a.rearrange("p (h n) -> p h n", h=2)
                    dve.scalar_tensor_tensor(view(zs), psA[:, :, 0:AW], HD ** -0.5, view(sbmask),
                                             ALU.mult, ALU.add).then_inc(zs_ready.sem, 1)

                def sb_keep(c):
                    dve.wait_ge(sp0_ready.sem, sp0_ready.at(l, c + 1))
                    dve.scalar_tensor_tensor(sp, zs, 0.0, sp, ALU.max, ALU.add).then_inc(sp_ready.sem, 1)

                def sb_between(c):
                    dve.wait_ge(b_done.sem, b_done.at(l, c + 1))
                    if c:
                        dve.wait_ge(a_ready.sem, a_ready.at(l, c))
                    view = lambda a: a.rearrange("p (h n) -> p h n", h=2)
                    dve.tensor_tensor(view(tt), psA[:, :, 0:AW], view(zs), ALU.add).then_inc(t_ready.sem, 1)

                input_lo(0, 0)
                split(G_CV + PER_TILE - 1)
                input_lo(0, 1)
                split(G_CV + PER_TILE - 1 + AHEAD)
                dve.wait_ge(par_in.sem, par_in.at(l, 0))
                dve.memset(gpad[:, :, 0:CV_K - 1], 0.0).then_inc(gpad_zero.sem, 1)
                for t in range(TOK):
                    dve.wait_ge(cv_sig.sem, cv_sig.at(l, t + 1))
                    dve.tensor_tensor(glu[:, t * CV_W:(t + 1) * CV_W], accs[0][t][:, 0:CV_W],
                                      sig[:, t * CV_W:(t + 1) * CV_W], ALU.mult).then_inc(cv_g.sem, 1)
                split(G_DLQ + 1 + AHEAD)
                conv_taps(1, 3)
                split(G_DLQ + 2 + AHEAD)
                conv_taps(3, 5)
                split(G_DLQ + 3 + AHEAD)
                rope(1, qr, G_DLQ + PER_TILE, q_roped)
                split(G_DLK + AHEAD)
                conv_taps(5, 7)
                split(G_DLK + 1 + AHEAD)
                conv_taps(7, 8)
                split(G_DLK + 2 + AHEAD)
                conv_taps(8, 10)
                split(G_DLK + 3 + AHEAD)
                rope(0, kr, G_DLK + PER_TILE, k_roped)
                split(G_DLV + AHEAD)
                conv_taps(10, 12)
                split(G_DLV + 1 + AHEAD)
                conv_taps(12, 13)
                split(G_DLV + 2 + AHEAD)
                conv_taps(13, 15)
                split(G_DLV + 3 + AHEAD)
                scores_max(0)
                split(G_SBQK + AHEAD)
                probabilities(0)
                scores_max(1)
                split(G_SBQK + 1 + AHEAD)
                probabilities(1)
                scores_max(2)
                split(G_SBQK + 2 + AHEAD)
                mixed_lo(1, 4, attended)
                probabilities(2)
                scores_max(3)
                split(G_SBQK + 3 + AHEAD)
                mixed_lo(2, 5, attended)
                probabilities(3)
                conv_taps(15, 17)
                split(G_SBV + AHEAD)
                mixed_lo(3, 6, attended)
                conv_taps(17, 19)
                split(G_SBV + 1 + AHEAD)
                split(G_WK1 + AHEAD)
                sb_masked(0)
                conv_taps(19, 23)
                sb_keep(0)
                mixed_lo(4, 7, attended)
                split(G_WK1 + 1 + AHEAD)
                conv_taps(23, 25)
                sb_between(0)
                split(G_WK1 + 2 + AHEAD)
                sb_masked(1)
                conv_taps(25, 28)
                split(G_WK1 + 3 + AHEAD)
                sb_keep(1)
                conv_taps(28, CV_K)
                split(G_WV0 + AHEAD)
                mixed_lo(5, 0, accs[0][0][:, 0:SEQ])
                for t in range(TOK):
                    dve.wait_ge(ln_tr.sem, ln_tr.at(l, t + 1))
                    own.link(dve.bn_stats(st(S_BN + 6 * t, 6), psCD[t][:, 0:CV_W]))
                    own.link(dve.bn_aggr(st(S_MV + 2 * t, 2), st(S_BN + 6 * t, 6)))
                    dve.tensor_scalar(st(S_LMS + t), st(S_MV + 2 * t + 1), EPS, None, ALU.add).then_inc(ln_ms.sem, 1)
                split(G_WV0 + 1 + AHEAD)
                for t in range(TOK):
                    dve.wait_ge(ln_rs.sem, ln_rs.at(l, t + 1))
                    dve.tensor_scalar(lnn[:, t * CV_W:(t + 1) * CV_W], psCD[t][:, 0:CV_W], st(S_MV + 2 * t),
                                      st(S_LRS + t), ALU.subtract, ALU.mult).then_inc(ln_n.sem, 1)
                sb_between(1)
                split(G_WV0 + 3 + AHEAD)
                for c in range(2):
                    mixed_lo(6 + c, 2 + c, psCD[c][:, 0:SEQ], par[:, PC_PWB + c:PC_PWB + c + 1])
                split(G_OUT + 1 + AHEAD)
                mixed_lo(8, 1, psCD[1][:, 0:SEQ])
                split(G_OUT + PER_TILE - 1 + AHEAD)
                output_first(0, 0, G_OUT + PER_TILE, 0)
                split(G_OUT + 2 * PER_TILE - 1)
                turn(0, [(1, 1, (3, 4))], G_OUT + 2 * PER_TILE)

                split(G_XQ + PER_TILE - 1)
                input_lo(1, 1)

                def cross_max(hd):
                    dve.wait_ge(xs_done.sem, xs_done.at(l, hd + 1))
                    b = hd % 2
                    own.link(dve.tensor_reduce(st(S_XMX + 2 * b, 2),
                                               psAB[b][:, :].rearrange("p (t n) -> p t n", t=TOK), AX_X, ALU.max))
                    dve.tensor_scalar(st(S_XNB + 2 * b, 2), st(S_XMX + 2 * b, 2), -(D // X_HEADS) ** -0.5, None,
                                      ALU.mult).then_inc(xnb.sem, 1)

                def cross_norm(hd):
                    dve.wait_ge(xe_done.sem, xe_done.at(l, hd + 1))
                    b = hd % 2
                    own.link(dve.reciprocal(st(S_XRD + 2 * b, 2), st(S_XDEN + 2 * b, 2)))
                    for t in range(TOK):
                        e = dve.tensor_scalar(xp[:, b, t, :], xp[:, b, t, :], st(S_XRD + 2 * b + t), None, ALU.mult)
                    e.then_inc(xp_ready.sem, 1)

                def crossed_lo(hd):
                    dve.wait_ge(xo_hi.sem, xo_hi.at(l, hd + 1))
                    cols = slice(hd * 2 * SEQ, (hd + 1) * 2 * SEQ)
                    dve.tensor_tensor(oT_lo[:, cols], psCD[1][:, :], oT_hi[:, cols].bitcast(F32),
                                      ALU.subtract).then_inc(xo_lo.sem, 1)

                split(G_XQ + PER_TILE + 2 + AHEAD)
                cross_max(0)
                cross_max(1)
                cross_norm(0)
                cross_norm(1)
                split(G_XQ + 2 * PER_TILE - 1 + AHEAD)
                cross_max(2)
                cross_norm(2)
                crossed_lo(0)
                cross_max(3)
                cross_norm(3)
                split(G_XO + AHEAD)
                crossed_lo(1)
                split(G_XO + 2 + AHEAD)
                crossed_lo(2)
                split(G_XO + 4 + AHEAD)
                crossed_lo(3)
                dve.wait_ge(gpost_in.sem, gpost_in.at(l, 1))
                turn(1, [(0, 0, (5, 7)), (1, 1, (6, 8))], G_XO + 2 * PER_TILE)
                split(G_UP + PER_TILE - 1)
                input_lo(2, 1)

                def up_taps(j):
                    y = ffy[j % 2]
                    dve.wait_ge(y_tap2.sem, y_tap2.at(l, j + 1))
                    for k in range(2):
                        for c in range(4):
                            fc = (FFC if c >= 2 else 0) + 2 * j + c % 2
                            u = psCD[c // 2][:, c % 2 * SEQ:(c % 2 + 1) * SEQ]
                            shift = k + 1
                            if k and c == 0:
                                dve.wait_ge(own.sem, own.n)
                            e = dve.scalar_tensor_tensor(y[:, c, shift:SEQ], u[:, 0:SEQ - shift],
                                                         par[:, PC_FW + 3 * fc + 1 - k:PC_FW + 3 * fc + 2 - k],
                                                         y[:, c, shift:SEQ], ALU.mult, ALU.add)
                            if k == 0 and c == 3:
                                own.n += 1
                                e.then_inc(own.sem, 1)
                    e.then_inc(y_conv.sem, 1)

                def gated(j):
                    y, g = ffy[j % 2], ffg[j % 2]
                    dve.wait_ge(gelu_done.sem, gelu_done.at(l, j + 1))
                    dve.tensor_tensor(g.rearrange("p (c n) -> p c n", c=2),
                                      g.rearrange("p (c n) -> p c n", c=2), y[:, 2:4, :], ALU.mult).then_inc(gv_done.sem, 1)

                def gated_lo(j):
                    cols = slice(2 * j * SEQ, 2 * (j + 1) * SEQ)
                    dve.wait_ge(g_hi.sem, g_hi.at(l, j + 1))
                    dve.tensor_tensor(gT_lo[:, cols], ffg[j % 2], gT_hi[:, cols].bitcast(F32), ALU.subtract).then_inc(g_lo.sem, 1)

                for j in range(UP_TILES):
                    split(G_UP + (j + 1) * PER_TILE + 1 + AHEAD)
                    up_taps(j)
                    split(G_UP + (j + 1) * PER_TILE + 2 + AHEAD)
                    gated(j)
                    gated_lo(j)
                split(G_DOWN + 6 + AHEAD)
                dve.wait_ge(gpre_in.sem, gpre_in.at(l, 3))
                memory_gain()
                split(G_DOWN + 7 + AHEAD)
                memory_lo(l, 0)
                split(G_DOWN + 9 + AHEAD)
                memory_lo(l, 1)
                split(G_DOWN + DOWN_GROUPS - 1 + AHEAD)
                output_first(2, 1, G_DOWN + DOWN_GROUPS, 2)
                split(GROUPS - 1)
                turn(2, [(1, 0, (11, 12))], GROUPS)
                own.clear()

        @block.tensor
        def _(pe):
            pe.nop().then_inc(w_used.sem, RING)
            pe.wait_ge(cst_in.sem, 16)

            def flip(dst, src, n=4):
                for i in range(n):
                    e = pe.transpose(dst[:, i * P:(i + 1) * P], src[:, i * P:(i + 1) * P], ident)
                return e

            def memory(l, t):
                pe.wait_ge(mg_done.sem, mg_done.at(l, t + 1))
                for b in range(2):
                    pe.wait_ge(mt_lo.sem, mt_lo.at(l, 2 * t + b - 1))
                    flip(psCD[b], xn[:, t * D + b * NT:t * D + (b + 1) * NT]).then_inc(mt_tr.sem, 1)

            for t in range(TOK):
                pe.wait_ge(mg_done.sem, mg_done.at(0, t - TOK + 1))
                for b in range(2):
                    if t:
                        pe.wait_ge(mt_lo.sem, mt_lo.at(0, b + 1 - 2 * TOK))
                    flip(psCD[b], xn[:, t * D + b * NT:t * D + (b + 1) * NT]).then_inc(mt_tr.sem, 1)
            pe.wait_ge(mt_lo.sem, mt_lo.at(0, 0))

            with pe.Fori(0, DEPTH) as l:
                def product(g0, groups, lhs, outs, k0=0, k_of=KC, width=NT, order=None):
                    hi, lo = lhs
                    per = GW // width
                    for g in range(g0, g0 + groups):
                        s = g % RING
                        pe.wait_ge(w_lo.sem, w_lo.at(l, g + 1))
                        for u in range(per):
                            k = k0 + (g - g0) * per + u
                            c = k if order is None else order[k]
                            cols = slice(s * GW + u * width, s * GW + (u + 1) * width)
                            for t in range(TOK):
                                a_hi = hi[:, c * SEQ + t * P:c * SEQ + (t + 1) * P]
                                a_lo = lo[:, c * SEQ + t * P:c * SEQ + (t + 1) * P]
                                pe.matmul(outs[t], a_hi, whi[:, cols], start=k == 0, stop=False)
                                pe.matmul(outs[t], a_hi, wlo[:, cols], start=False, stop=False)
                                e = pe.matmul(outs[t], a_lo, whi[:, cols], start=False, stop=k == k_of - 1)
                        e.then_inc(w_used.sem, 1)

                def first_product(i, g0, lhs, outs):
                    hi, lo = lhs
                    for t in range(TOK):
                        for g in range(g0, g0 + PER_TILE):
                            s = g % RING
                            if t == 0:
                                pe.wait_ge(w_lo.sem, w_lo.at(l, g + 1))
                                if g == g0 + PER_TILE - 1 and i < 2:
                                    inputs(i, 1)
                            if (g - g0) * UNITS % 4 == 0:
                                pe.wait_ge(xt_lo.sem, xt_lo.at(l, 2 * TOK * i + 2 * t + (g - g0) * UNITS // 4 + 1))
                            for u in range(UNITS):
                                k = (g - g0) * UNITS + u
                                cols = slice(s * GW + u * NT, s * GW + (u + 1) * NT)
                                a_hi = hi[:, k * SEQ + t * P:k * SEQ + (t + 1) * P]
                                a_lo = lo[:, k * SEQ + t * P:k * SEQ + (t + 1) * P]
                                pe.matmul(outs[t], a_hi, whi[:, cols], start=k == 0, stop=False)
                                pe.matmul(outs[t], a_hi, wlo[:, cols], start=False, stop=False)
                                e = pe.matmul(outs[t], a_lo, whi[:, cols], start=False, stop=k == KC - 1)
                            if t == TOK - 1:
                                e.then_inc(w_used.sem, 1)
                        if t == 0 and i == 2:
                            inputs(i, 1)

                def last_product(steps, lhs, k_of, order=None, heads_end=None):
                    hi, lo = lhs
                    for t in range(TOK):
                        for g, k0, outs, ends in steps if not t else sorted(steps):
                            if not t:
                                pe.wait_ge(w_lo.sem, w_lo.at(l, g + 1))
                                if heads_end == k0 + UNITS:
                                    pe.wait_ge(xo_lo.sem, xo_lo.at(l, X_HEADS))
                            s = g % RING
                            for u in range(UNITS):
                                c = k0 + u if order is None else order[k0 + u]
                                cols = slice(s * GW + u * NT, s * GW + (u + 1) * NT)
                                a_hi = hi[:, c * SEQ + t * P:c * SEQ + (t + 1) * P]
                                a_lo = lo[:, c * SEQ + t * P:c * SEQ + (t + 1) * P]
                                pe.matmul(acc[outs][t], a_hi, whi[:, cols], start=False, stop=False)
                                pe.matmul(acc[outs][t], a_hi, wlo[:, cols], start=False, stop=False)
                                e = pe.matmul(acc[outs][t], a_lo, whi[:, cols], start=False,
                                              stop=k0 + u == k_of - 1)
                            if t:
                                e.then_inc(w_used.sem, 1)
                            elif ends:
                                e.then_inc(y_tile0.sem, 1)

                X, O, M = (xT_hi, xT_lo), (oT_hi, oT_lo), (mT_hi, mT_lo)
                acc = [[accs[s][t][:, :] for t in range(TOK)] for s in range(2)]

                def inputs(i, t):
                    for b in range(2):
                        pe.wait_ge(xn_ready.sem, xn_ready.at(l, 2 * (TOK * i + t) + b + 1))
                        if t:
                            pe.wait_ge(xt_lo.sem, xt_lo.at(l, 2 * TOK * i + b + 1))
                        flip(psCD[b], xn[:, t * D + b * NT:t * D + (b + 1) * NT]).then_inc(xt_tr.sem, 1)

                def rows_to_columns(src, ready, n0, done, n=4):
                    for t in range(TOK):
                        pe.wait_ge(ready.sem, ready.at(l, n0 + t + 1))
                        flip(psCD[t], src[:, t * n * P:(t + 1) * n * P], n).then_inc(done.sem, 1)

                def dl_scores(c):
                    for r in range(2):
                        if c:
                            pe.wait_ge(nb_ready.sem, nb_ready.at(l, 2 * (c - 1) + r + 1))
                        q, k = (a[r * HD:(r + 1) * HD, c, :] for a in (dqT, dkT))
                        pe.matmul(psAB[r][:, 0:P], q[:, 0:P], k[:, 0:P], start=True, stop=True)
                        pe.matmul(psAB[r][:, P:AW], q[:, P:SEQ], k, start=True, stop=True).then_inc(s_done.sem, 1)

                def dl_flip(c):
                    for r in range(2):
                        pe.wait_ge(p_ready.sem, p_ready.at(l, 2 * c + r + 1))
                        flip(psCD[r], sms[c % 2][r], 3).then_inc(p_tr.sem, 1)

                def dl_values(c):
                    pe.wait_ge(pT_in.sem, pT_in.at(l, 2 * c + 2))
                    for r in range(2):
                        o, v0 = accs[1][1][r * HD:(r + 1) * HD, :], (2 * c + r) * HD
                        pe.matmul(o[:, 0:SEQ], dlv[:, v0:v0 + HD], pT[:, r, 0:SEQ], start=True, stop=False)
                        e = pe.matmul(o[:, P:SEQ], dlv[:, NT + v0:NT + v0 + HD], pT[:, r, SEQ:AW],
                                      start=False, stop=True)
                    e.then_inc(o_done.sem, 1)

                def sb_scores(c):
                    for r in range(2):
                        q, k = (sbT[r * HD:(r + 1) * HD, i + c, :] for i in (0, 2))
                        pe.matmul(psAB[r][:, 0:SEQ], k[:, 0:P], q, start=True, stop=True)
                        e = pe.matmul(psAB[r][:, SEQ:AW], k[:, P:SEQ], q[:, P:SEQ], start=True, stop=True)
                    e.then_inc(z_done.sem, 1)

                def sb_between(c):
                    pe.wait_ge(sp_ready.sem, sp_ready.at(l, c + 1))
                    for r in range(2):
                        k = sp[:, r * AW:(r + 1) * AW]
                        pe.matmul(psAB[r][:, 0:SEQ], tri, k[:, 0:SEQ], start=True, stop=False)
                        pe.matmul(psAB[r][:, P:SEQ], ones, k[:, SEQ:AW], start=False, stop=True)
                        e = pe.matmul(psAB[r][:, SEQ:AW], tri, k[:, SEQ:AW], start=True, stop=True)
                    e.then_inc(b_done.sem, 1)

                def sb_values(c, bank):
                    pe.wait_ge(a_ready.sem, a_ready.at(l, c + 1))
                    for r in range(2):
                        o, v0 = bank[r * HD:(r + 1) * HD, :], (2 * c + r) * HD
                        a = sb_w[c][:, r * AW:(r + 1) * AW]
                        pe.matmul(o[:, 0:SEQ], sbv[:, v0:v0 + HD], a[:, 0:SEQ], start=True, stop=False)
                        e = pe.matmul(o[:, P:SEQ], sbv[:, SB_W + v0:SB_W + v0 + HD], a[:, SEQ:AW],
                                      start=False, stop=True)
                    e.then_inc(sbo_done.sem, 1)

                product(G_WK0, 2, M, psAB)
                inputs(0, 0)
                product(G_WK0 + 2, 2, M, psAB, k0=4)
                first_product(0, G_CV, X, acc[0])
                rows_to_columns(ktok, k_in, 0, k_tr)
                product(G_DLQ, 2, X, acc[1])
                pe.wait_ge(KT_in.sem, KT_in.at(l, TOK))
                rows_to_columns(glu, cv_g, 0, g_tr, 2)
                product(G_DLQ + 2, 2, X, acc[1], k0=4)
                product(G_DLK, 2, X, acc[0])
                pe.wait_ge(gpad_in.sem, gpad_in.at(l, TOK))
                rows_to_columns(qr, q_roped, 0, q_tr)
                product(G_DLK + 2, 2, X, acc[0], k0=4)
                product(G_DLV, 2, X, acc[1])
                pe.wait_ge(dqT_in.sem, dqT_in.at(l, TOK))
                rows_to_columns(kr, k_roped, 0, kr_tr)
                product(G_DLV + 2, 2, X, acc[1], k0=4)
                pe.wait_ge(dkT_in.sem, dkT_in.at(l, TOK))
                pe.wait_ge(k_in.sem, k_in.at(l, TOK))
                dl_scores(0)
                product(G_SBQK, 1, X, acc[0])
                dl_scores(1)
                product(G_SBQK + 1, 1, X, acc[0], k0=2)
                dl_flip(0)
                dl_scores(2)
                pe.wait_ge(dlv_in.sem, dlv_in.at(l, TOK))
                product(G_SBQK + 2, 1, X, acc[0], k0=4)
                dl_values(0)
                dl_flip(1)
                dl_scores(3)
                product(G_SBQK + 3, 1, X, acc[0], k0=6)
                pe.wait_ge(mix_lo.sem, mix_lo.at(l, 1))
                dl_values(1)
                dl_flip(2)

                def stick_values(t):
                    for g in range(G_SBV, G_SBV + PER_TILE // 2):
                        if not t:
                            pe.wait_ge(w_lo.sem, w_lo.at(l, g + 1))
                        for u in range(2 * UNITS):
                            k = (g - G_SBV) * 2 * UNITS + u
                            cols = slice(g % RING * GW + u * SB_W, g % RING * GW + (u + 1) * SB_W)
                            dst = accs[1][0][:, t * SB_W:(t + 1) * SB_W]
                            a_hi = xT_hi[:, k * SEQ + t * P:k * SEQ + (t + 1) * P]
                            a_lo = xT_lo[:, k * SEQ + t * P:k * SEQ + (t + 1) * P]
                            pe.matmul(dst, a_hi, whi[:, cols], start=k == 0, stop=False)
                            pe.matmul(dst, a_hi, wlo[:, cols], start=False, stop=False)
                            e = pe.matmul(dst, a_lo, whi[:, cols], start=False, stop=k == KC - 1)
                        if t:
                            e.then_inc(w_used.sem, 1)

                stick_values(0)
                pe.wait_ge(mix_lo.sem, mix_lo.at(l, 2))
                dl_values(2)
                rows_to_columns(sbst, sbst_in, 0, sb_tr)
                stick_values(1)
                pe.wait_ge(sbT_in.sem, sbT_in.at(l, TOK))
                dl_flip(3)
                pe.wait_ge(nb_ready.sem, nb_ready.at(l, DL_HEADS))
                sb_scores(0)
                product(G_WK1, 1, M, acc[0])
                pe.wait_ge(mix_lo.sem, mix_lo.at(l, 3))
                dl_values(3)
                product(G_WK1 + 1, 1, M, acc[0], k0=2)
                sb_between(0)
                product(G_WK1 + 2, 1, M, acc[0], k0=4)
                pe.wait_ge(t_ready.sem, t_ready.at(l, 1))
                sb_scores(1)
                product(G_WK1 + 3, 1, M, acc[0], k0=6)
                pe.wait_ge(sbv_in.sem, sbv_in.at(l, 1))
                pe.wait_ge(mix_lo.sem, mix_lo.at(l, 4))
                product(G_WV0, 1, M, acc[1])
                pe.wait_ge(k_in.sem, k_in.at(l, 2 * TOK))
                sb_values(0, accs[0][0])
                for t in range(TOK):
                    for c in range(2):
                        pe.wait_ge(conv_done.sem, conv_done.at(l, c + 1))
                        e = pe.transpose(psCD[t][:, c * P:(c + 1) * P],
                                         cacc[:, c * SEQ + t * P:c * SEQ + (t + 1) * P], ident)
                    e.then_inc(ln_tr.sem, 1)
                product(G_WV0 + 1, 1, M, acc[1], k0=2)
                sb_between(1)
                product(G_WV0 + 2, 1, M, acc[1], k0=4)
                pe.wait_ge(ln_n.sem, ln_n.at(l, TOK))
                for c in range(2):
                    for t in range(TOK):
                        e = pe.transpose(psCD[c][:, t * P:(t + 1) * P], lnn[:, t * CV_W + c * P:t * CV_W + (c + 1) * P],
                                         ident)
                    e.then_inc(ln_tb.sem, 1)
                product(G_WV0 + 3, 1, M, acc[1], k0=6)
                pe.wait_ge(silu.sem, silu.at(l, 2))
                for co in range(2):
                    for ci in range(2):
                        e = pe.matmul(psCD[co][:, 0:SEQ], pww[:, ci * CV_W + co * P:ci * CV_W + (co + 1) * P],
                                      sil[:, ci * SEQ:(ci + 1) * SEQ], start=ci == 0, stop=ci == 1)
                    e.then_inc(pw_done.sem, 1)
                pe.wait_ge(mix_lo.sem, mix_lo.at(l, 5))
                product(G_OUT, 1, O, acc[0], order=MIX_ORDER)
                pe.wait_ge(mix_lo.sem, mix_lo.at(l, 7))
                rows_to_columns(ktok, k_in, TOK, k_tr)
                product(G_OUT + 1, 1, O, acc[0], k0=2, order=MIX_ORDER)
                pe.wait_ge(KT_in.sem, KT_in.at(l, 2 * TOK))
                sb_values(1, psCD[1])
                product(G_OUT + 2, 1, O, acc[0], k0=4, order=MIX_ORDER)
                pe.wait_ge(mix_lo.sem, mix_lo.at(l, KC))
                product(G_OUT + 3, 1, O, acc[0], k0=6, order=MIX_ORDER)
                pe.wait_ge(V_in.sem, V_in.at(l, TOK))
                product(G_OUT + PER_TILE, 1, O, acc[1], order=MIX_ORDER)
                last_product([(G_OUT + PER_TILE + j, 2 * j, 1, j == 3) for j in range(1, 4)], O, KC, MIX_ORDER)
                product(G_WV1, 2, M, psAB)
                inputs(1, 0)
                product(G_WV1 + 2, 2, M, psAB, k0=4)

                def x_scores(hd):
                    if hd >= 2:
                        pe.wait_ge(xe_done.sem, xe_done.at(l, hd - 1))
                    for t in range(TOK):
                        for i in range(2):
                            e = pe.matmul(psAB[hd % 2][:, t * SEQ:(t + 1) * SEQ], qT[:, 2 * hd + i, t * P:(t + 1) * P],
                                          KT[:, (2 * hd + i) * SEQ:(2 * hd + i + 1) * SEQ], start=i == 0, stop=i == 1)
                    e.then_inc(xs_done.sem, 1)

                def x_flip(hd):
                    pe.wait_ge(xp_ready.sem, xp_ready.at(l, hd + 1))
                    for m in range(2):
                        for t in range(TOK):
                            e = pe.transpose(psCD[0][:, m * SEQ + t * P:m * SEQ + (t + 1) * P],
                                             xp[:, hd % 2, t, m * P:(m + 1) * P], ident)
                    e.then_inc(xp_tr.sem, 1)

                def x_values(hd):
                    pe.wait_ge(xpT_in.sem, xpT_in.at(l, hd + 1))
                    if hd:
                        pe.wait_ge(xo_lo.sem, xo_lo.at(l, hd))
                    for i in range(2):
                        for m in range(2):
                            v0 = m * D + (2 * hd + i) * P
                            e = pe.matmul(psCD[1][:, i * SEQ:(i + 1) * SEQ], V[:, v0:v0 + P],
                                          xpT[:, m * SEQ:(m + 1) * SEQ], start=m == 0, stop=m == 1)
                    e.then_inc(xo_done.sem, 1)

                first_product(1, G_XQ, X, acc[0])
                product(G_XQ + PER_TILE, 2, X, acc[1])
                rows_to_columns(xn[:, 0:TOK * NT], qx_in, 0, qx_tr)
                product(G_XQ + PER_TILE + 2, 1, X, acc[1], k0=4)
                pe.wait_ge(qT_in.sem, qT_in.at(l, TOK))
                pe.wait_ge(V_in.sem, V_in.at(l, 2 * TOK))
                x_scores(0)
                x_scores(1)
                product(G_XQ + PER_TILE + 3, 1, X, acc[1], k0=6)
                rows_to_columns(xn[:, TOK * NT:2 * TOK * NT], qx_in, TOK, qx_tr)
                pe.wait_ge(qT_in.sem, qT_in.at(l, 2 * TOK))
                x_flip(0)
                x_scores(2)
                x_values(0)
                x_flip(1)
                x_scores(3)

                def wo(hd, n):
                    product(G_XO + 2 * hd + n, 1, O, acc[n], k0=2 * hd)

                pe.wait_ge(xo_lo.sem, xo_lo.at(l, 1))
                wo(0, 0)
                x_values(1)
                x_flip(2)
                wo(0, 1)
                pe.wait_ge(xo_lo.sem, xo_lo.at(l, 2))
                wo(1, 0)
                x_values(2)
                x_flip(3)
                wo(1, 1)
                pe.wait_ge(xo_lo.sem, xo_lo.at(l, 3))
                x_values(3)
                g = G_XO + PER_TILE
                last_product([(g, 4, 0, False), (g + 2, 4, 1, False), (g + 1, 6, 0, True), (g + 3, 6, 1, True)], O, KC,
                             heads_end=KC)
                inputs(2, 0)

                def up_flip(j):
                    if j:
                        pe.wait_ge(y_conv.sem, y_conv.at(l, j))
                    pe.wait_ge(u_in.sem, u_in.at(l, TOK * (j + 1)))
                    for b in range(2):
                        for c in range(2):
                            for t in range(TOK):
                                col = t * NT + (2 * b + c) * P
                                e = pe.transpose(psCD[b][:, c * SEQ + t * P:c * SEQ + (t + 1) * P],
                                                 ust[j % 2][:, col:col + P], ident)
                        e.then_inc(u_tr.sem, 1)

                for j in range(UP_TILES):
                    if j >= 2:
                        pe.wait_ge(u_in.sem, u_in.at(l, TOK * (j - 1)))
                    if not j:
                        first_product(2, G_UP, X, acc[0])
                        continue
                    product(G_UP + j * PER_TILE, 2, X, acc[j % 2])
                    if j:
                        up_flip(j - 1)
                    product(G_UP + j * PER_TILE + 2, 2, X, acc[j % 2], k0=4)
                G = (gT_hi, gT_lo)
                pe.wait_ge(u_in.sem, u_in.at(l, TOK * (UP_TILES - 1)))
                for g in range(DOWN_GROUPS):
                    pe.wait_ge(g_lo.sem, g_lo.at(l, g + 1))
                    product(G_DOWN + g, 1, G, acc[1], k0=2 * g, k_of=FFC)
                    if g == 1:
                        up_flip(UP_TILES - 1)
                    if g == 7:
                        memory(l, 0)
                    if g == 9:
                        memory(l, 1)
                g, last = G_DOWN + DOWN_GROUPS, DOWN_GROUPS - RING
                product(g, last, G, acc[0], k_of=FFC)
                last_product([(g + j, 2 * j, 0, j == DOWN_GROUPS - 1) for j in range(last, DOWN_GROUPS)], G, FFC)

    return nc


def _weight_groups(a):
    def tiles(w, width=NT):
        k, n = w.shape
        per = GW // width
        v = w.reshape(k // P // per, per, P, n // width, width)
        return v.transpose(3, 0, 2, 1, 4).reshape(-1, P, GW)

    layers = []
    for l in range(DEPTH):
        w_in = a["w_in"][l]
        cv = 3 * SB_W
        dl = cv + 2 * CV_W
        k, v = tiles(a["x_wk"][l]), tiles(a["x_wv"][l])
        up = a["ffn_w_up"][l].reshape(D, 2, FFC // 2, 2 * P).transpose(0, 2, 1, 3).reshape(D, 2 * D_FF)
        w_out = a["w_out"][l].reshape(KC, P, D)[list(MIX_ORDER)].reshape(D, D)
        wo = tiles(a["x_wo"][l])[[0, 4, 1, 5, 2, 3, 6, 7]]
        layers += [k[:PER_TILE], tiles(w_in[:, cv:dl]), tiles(w_in[:, dl:]), tiles(w_in[:, 0:2 * SB_W]),
                   tiles(w_in[:, 2 * SB_W:cv], SB_W), k[PER_TILE:], v[:PER_TILE], tiles(w_out),
                   v[PER_TILE:], tiles(a["x_wq"][l]), wo, tiles(up), tiles(a["ffn_w_down"][l])]
    return np.ascontiguousarray(np.concatenate(layers))


def _by_feature(v, n):
    v = v.reshape(-1, n, P)
    return v.transpose(2, 1, 0).reshape(P, -1)


def _params(a):
    rows = []
    for l in list(range(DEPTH)) + [0]:
        rows.append(np.concatenate([
            _by_feature(a["cv_w"][l], 2), _by_feature(a["cv_b"][l], 2), _by_feature(a["cv_ln_g"][l], 2),
            _by_feature(a["cv_ln_b"][l], 2), _by_feature(a["cv_pw_b"][l], 2),
            _by_feature(a["ffn_conv_w"][l], 2 * FFC), _by_feature(a["ffn_conv_b"][l], 2 * FFC)], axis=1))
    return np.stack(rows)


def _gains(a):
    names = ["mem_norm", "mix_norm_pre", "mix_norm_post", "x_norm_pre", "x_norm_post", "ffn_norm_pre",
             "ffn_norm_post"]
    g = np.stack([a[n] for n in names], axis=1)
    return np.concatenate([g, g[:1]])


def _constants():
    c = np.zeros((P, CC), np.float32)
    i, j = np.arange(P)[:, None], np.arange(P)[None, :]
    c[:, CC_ID:CC_ID + P] = i == j
    c[:, CC_TRI:CC_TRI + P] = -(i >= j).astype(np.float32)
    c[:, CC_ONE:CC_ONE + P] = -1.0
    before = np.concatenate([np.arange(SEQ)[None, :] > i, j > i], axis=1)
    c[:, CC_SB:CC_SB + 2 * AW] = np.where(np.concatenate([before, before], axis=1), 0.0, -3e38)
    dist = np.concatenate([i - j, i + P - np.arange(SEQ)[None, :]], axis=1)
    count = sum(((dist >= 0) & (dist % d == 0) & (dist <= w)).astype(np.float32)
                for w, d in ((128, 1), (512, 4), (2048, 16)))
    c[:, CC_NEG:CC_NEG + AW] = np.where(count > 0, 0.0, -3e38)
    c[:, CC_MUL:CC_MUL + AW] = count
    c[:, CC_FRQ:CC_FRQ + HALF] = np.float32(10000.0) ** (-np.arange(HALF, dtype=np.float32) / np.float32(HALF))
    return c


def kernel(**inputs):
    import concourse.bacc as bacc
    from concourse.bass_utils import run_bass_kernel_spmd

    a = {k: np.asarray(v) for k, v in inputs.items()}
    arrays = {
        "x_dram": a["x"][0], "mem_dram": a["mem"][0],
        "pos_dram": a["positions"].reshape(TOK, P).T,
        "const_dram": _constants(), "gain_dram": _gains(a), "param_dram": _params(a),
        "pw_dram": np.concatenate([a["cv_pw_w"], a["cv_pw_w"][:1]])
                     .reshape(DEPTH + 1, 2, P, CV_W).transpose(0, 2, 1, 3).reshape(DEPTH + 1, P, 2 * CV_W),
        "stream_dram": _weight_groups(a),
    }
    arrays = {k: np.ascontiguousarray(v) for k, v in arrays.items()}
    nc = bacc.Bacc("TRN2", target_bir_lowering=False, num_devices=1)
    aps = [nc.dram_tensor(n, v.shape, mybir.dt.from_np(v.dtype), kind="ExternalInput").ap()
           for n, v in arrays.items()]
    out = nc.dram_tensor("out_dram", (SEQ, D), F32, kind="ExternalOutput").ap()
    hybrid_trunk(nc, *aps, out)
    r = run_bass_kernel_spmd(nc, [arrays], core_ids=[0])
    return r.results[0]["out_dram"].reshape(1, SEQ, D)
```

```python
from contextlib import ExitStack

import numpy as np

import concourse.bass as bass
from concourse import mybir

F32 = mybir.dt.float32
F32R = mybir.dt.float32r
BF16 = mybir.dt.bfloat16
I32 = mybir.dt.int32
ACT = mybir.ActivationFunctionType
ALU = mybir.AluOpType
AX_X = mybir.AxisListType.X

P = 128
DEPTH = 2
D = 1024
SEQ = 256
TOK = SEQ // P
KC = D // P
HD = 64
SB_W, CV_W, DL_W = 256, 256, 512
DL_HEADS = DL_W // HD
CV_K = 31
D_FF = 2816
FFC = D_FF // P
X_HEADS = 4
EPS = 1e-6
NT = 512
HALF = HD // 2

UNITS = 2
GW = UNITS * NT
PER_TILE = KC // UNITS
UP_TILES = 2 * D_FF // NT
DOWN_GROUPS = FFC // UNITS
G_WK0 = 0
G_IN = G_WK0 + PER_TILE
G_DLQ, G_CV, G_DLK, G_DLV, G_SBQK, G_SBV = (G_IN + i * PER_TILE for i in range(6))
G_WK1 = G_SBV + PER_TILE // 2
G_WV0 = G_WK1 + PER_TILE
G_OUT = G_WV0 + PER_TILE
G_WV1 = G_OUT + 2 * PER_TILE
G_XQ = G_WV1 + PER_TILE
G_XO = G_XQ + 2 * PER_TILE
G_UP = G_XO + 2 * PER_TILE
G_DOWN = G_UP + UP_TILES * PER_TILE
GROUPS = G_DOWN + 2 * DOWN_GROUPS
RING = 4
AHEAD = RING - 1

MIX_ORDER = (4, 5, 6, 7, 0, 1, 2, 3)

PC_CVW = 0
PC_CVB = PC_CVW + 2 * CV_K
PC_LNG = PC_CVB + 2
PC_LNB = PC_LNG + 2
PC_PWB = PC_LNB + 2
PC_FW = PC_PWB + 2
PC_FB = PC_FW + 3 * 2 * FFC
PC = PC_FB + 2 * FFC

AW = 3 * P
CC_ID = 0
CC_FRQ = CC_ID + P
CC_TRI = CC_FRQ + HALF
CC_ONE = CC_TRI + P
CC_SB = CC_ONE + P
CC_NEG = CC_SB + 2 * AW
CC_MUL = CC_NEG + AW
CC = CC_MUL + AW

MEM_G, MIX_PRE, MIX_POST, X_PRE, X_POST, FFN_PRE, FFN_POST = range(7)


class Chain:

    def __init__(self, engine, sem):
        self.engine, self.sem, self.n = engine, sem, 0

    def link(self, instruction):
        self.n += 1
        instruction.then_inc(self.sem, 1)
        self.engine.wait_ge(self.sem, self.n)

    def clear(self):
        if self.n:
            self.engine.sem_clear(self.sem)
        self.n = 0


class Signal:

    def __init__(self, sem, per_layer, before=0, unit=1):
        self.sem, self.per_layer, self.before, self.unit = sem, per_layer, before, unit

    def at(self, layer, n):
        return (layer * self.per_layer + (self.before + n)) * self.unit


def hybrid_trunk(nc, x, mem, pos, consts, gains, params, pw, stream, out):
    with ExitStack() as ctx:
        def sb(name, cols, dt=F32):
            return ctx.enter_context(nc.sbuf_tensor(name, [P, cols], dt))

        def signal(name, per_layer, before=0, unit=1):
            return Signal(ctx.enter_context(nc.semaphore(name)), per_layer, before, unit)

        raw = sb("raw", RING * GW)
        whi = sb("whi", RING * GW, F32R)
        wlo = sb("wlo", RING * GW, F32R)
        h = sb("h", TOK * D)
        xn = sb("xn", TOK * D)
        xT_hi = sb("xT_hi", KC * SEQ, F32R)
        xT_lo = sb("xT_lo", KC * SEQ, F32R)
        oT_hi = sb("oT_hi", KC * SEQ, F32R)
        oT_lo = sb("oT_lo", KC * SEQ, F32R)
        mT_hi = sb("mT_hi", KC * SEQ, F32R)
        mT_lo = sb("mT_lo", KC * SEQ, F32R)
        memn = sb("memn", TOK * D)
        KT = sb("KT", KC * SEQ)
        V = sb("V", TOK * D)
        gpre = sb("gpre", D)
        gpost = sb("gpost", D)
        par = sb("par", PC)
        pww = sb("pww", 2 * CV_W)
        cst = sb("cst", CC)
        trig = sb("trig", TOK * 2 * HALF)
        stat = sb("stat", 96)
        posi = sb("posi", TOK, I32)
        zero = sb("zero", 2, F32R)
        junk = sb("junk", TOK * D, BF16)
        g_bytes = FFC * SEQ * 4
        ARENA = 48 * 1024 // 4
        base = nc.sbuf_base
        arena = sb("arena", ARENA)
        gT_hi = nc.alloc_sbuf_tensor_at("gT_hi", [P, FFC * SEQ], F32R, offset=base)
        gT_lo = nc.alloc_sbuf_tensor_at("gT_lo", [P, FFC * SEQ], F32R, offset=base + g_bytes)
        assert 2 * g_bytes <= ARENA * 4

        taken = [0]

        def part(cols):
            taken[0] += cols
            assert taken[0] <= ARENA, taken[0] - ARENA
            return arena[:, taken[0] - cols:taken[0]]

        gpad = part(2 * (CV_K - 1 + SEQ)).rearrange("p (c n) -> p c n", c=2)
        cacc = part(2 * SEQ)
        lnn = part(TOK * CV_W)
        sil = sig = part(2 * SEQ)
        sb_a = part(4 * 2 * AW)
        zs, sp, tt = (sb_a[:, i * 2 * AW:(i + 1) * 2 * AW] for i in range(3))
        qr, kr = sb_a[:, 0:TOK * NT], sb_a[:, TOK * NT:2 * TOK * NT]
        ra, rb = sb_a[:, 2 * TOK * NT:2 * TOK * NT + NT], sb_a[:, 2 * TOK * NT + NT:2 * TOK * NT + 2 * NT]
        dqT = part(4 * SEQ).rearrange("p (c n) -> p c n", c=4)
        dkT = part(4 * SEQ).rearrange("p (c n) -> p c n", c=4)
        dlv = part(TOK * NT)
        sbT = part(4 * SEQ).rearrange("p (c n) -> p c n", c=4)
        sbv = part(TOK * SB_W)
        sm0 = part(2 * AW)
        sms = [[sm0[:, 0:AW], sm0[:, AW:2 * AW]], [V[:, NT:NT + AW], V[:, D + NT:D + NT + AW]]]
        pT = part(2 * AW).rearrange("p (h n) -> p h n", h=2)
        sb_w = [a.rearrange("p c n -> p (c n)")[:, 0:2 * AW] for a in (dqT, dkT)]
        rows = xn[:, 0:TOK * NT]
        taken[0] = 0
        qT = part(KC * SEQ).rearrange("p (c n) -> p c n", c=KC)
        xp = part(2 * TOK * SEQ).rearrange("p (b t n) -> p b t n", b=2, t=TOK)
        xpT = part(2 * SEQ)
        ffy = [KT[:, b * 4 * SEQ:(b + 1) * 4 * SEQ].rearrange("p (c n) -> p c n", c=4) for b in range(2)]
        ffg = [V[:, b * 2 * SEQ:(b + 1) * 2 * SEQ] for b in range(2)]

        def bank(name):
            return ctx.enter_context(nc.psum_tensor(name, [P, NT], F32))

        accs = [[bank(f"acc{s}{t}") for t in range(TOK)] for s in range(2)]
        psA = ctx.enter_context(nc.psum_tensor("psAB", [P, 2, NT], F32))
        psAB = [psA[:, 0], psA[:, 1]]
        psC = ctx.enter_context(nc.psum_tensor("psCD", [P, 2, NT], F32))
        psCD = [psC[:, 0], psC[:, 1]]

        up_banks = [[accs[0][0], accs[0][1], accs[1][0], accs[1][1]], psAB + psCD]

        def up_chunk(j, c):
            return up_banks[j % 2][c][:, 0:SEQ] if j else accs[1][c // 2][:, c % 2 * SEQ:(c % 2 + 1) * SEQ]

        attended = accs[1][1][:, 0:SEQ]

        y_banks = [[a[:, :] for a in accs[0]], [a[:, :] for a in accs[1]], psAB]

        ident = cst[:, CC_ID:CC_ID + P]
        tri = cst[:, CC_TRI:CC_TRI + P]
        ones = cst[:, CC_ONE:CC_ONE + P]
        sbmask = cst[:, CC_SB:CC_SB + 2 * AW]
        negm = cst[:, CC_NEG:CC_NEG + AW]
        mult = cst[:, CC_MUL:CC_MUL + AW]

        raw_in = [signal(f"raw_in{s}", GROUPS // RING, unit=16) for s in range(RING)]
        w_hi = signal("w_hi", GROUPS)
        w_lo = signal("w_lo", GROUPS)
        w_used = signal("w_used", GROUPS, before=RING)
        mem0_in = signal("mem0_in", 0, before=1, unit=16)
        mem1_in = signal("mem1_in", 0, before=1, unit=16)
        head_in = signal("head_in", 0, before=1, unit=16)
        cst_in = signal("cst_in", 0, before=1, unit=16)
        x_in = signal("x_in", 0, before=1, unit=16)
        pos_in = signal("pos_in", 0, before=1, unit=16)
        trig_arg = signal("trig_arg", 0, before=1)
        trig_ready = signal("trig_ready", 0, before=1)
        mgain_in = signal("mgain_in", 0, before=1, unit=16)
        gpre_in = signal("gpre_in", 4, before=1, unit=16)
        gpost_in = signal("gpost_in", 3, before=1, unit=16)
        par_in = signal("par_in", 2, before=2, unit=16)
        mem_sq = signal("mem_sq", 0, before=TOK)
        mem_ms = signal("mem_ms", 0, before=TOK)
        mem_rs = signal("mem_rs", 0, before=TOK)
        mg_done = signal("mg_done", TOK, before=TOK)
        mt_tr = signal("mt_tr", 2 * TOK, before=2 * TOK)
        mt_hi = signal("mt_hi", 2 * TOK, before=2 * TOK)
        mt_lo = signal("mt_lo", 2 * TOK, before=2 * TOK)
        h_ready = signal("h_ready", 3 * 2 * TOK, before=2 * TOK)
        h_sq = signal("h_sq", 3 * 2 * TOK)
        h_ms = signal("h_ms", 3 * TOK)
        h_rs = signal("h_rs", 3 * TOK)
        xn_ready = signal("xn_ready", 3 * 2 * TOK)
        xt_tr = signal("xt_tr", 3 * 2 * TOK)
        xt_hi = signal("xt_hi", 3 * 2 * TOK)
        xt_lo = signal("xt_lo", 3 * 2 * TOK)
        y_tile0 = signal("y_tile0", 4)
        y_sq = signal("y_sq", 3 * 2 * TOK)
        y_ms = signal("y_ms", 3 * TOK)
        y_rs = signal("y_rs", 3 * TOK)
        KT_in = signal("KT_in", 4)
        V_in = signal("V_in", 2 * TOK)
        cv_sig = signal("cv_sig", 1)
        gpad_zero = signal("gpad_zero", 1)
        gpad_in = signal("gpad_in", 1)
        tap0 = signal("tap0", 2)
        conv_done = signal("conv_done", 2)
        ln_tr = signal("ln_tr", TOK)
        ln_ms = signal("ln_ms", TOK)
        ln_rs = signal("ln_rs", TOK)
        ln_n = signal("ln_n", TOK)
        ln_tb = signal("ln_tb", 2)
        silu = signal("silu", 2)
        pw_done = signal("pw_done", 2)
        q_roped = signal("q_roped", TOK)
        k_roped = signal("k_roped", TOK)
        q_tr = signal("q_tr", TOK)
        kr_tr = signal("kr_tr", TOK)
        dqT_in = signal("dqT_in", TOK)
        dkT_in = signal("dkT_in", TOK)
        dlv_in = signal("dlv_in", TOK)
        sbT_in = signal("sbT_in", 2)
        sbv_in = signal("sbv_in", 1)
        s_done = signal("s_done", DL_HEADS)
        nb_ready = signal("nb_ready", DL_HEADS)
        exp_done = signal("exp_done", DL_HEADS)
        den_ready = signal("den_ready", DL_HEADS)
        p_ready = signal("p_ready", DL_HEADS)
        p_tr = signal("p_tr", DL_HEADS)
        pT_in = signal("pT_in", DL_HEADS)
        o_done = signal("o_done", DL_HEADS // 2)
        z_done = signal("z_done", 2)
        zs_ready = signal("zs_ready", 2)
        sp0_ready = signal("sp0_ready", 2)
        sp_ready = signal("sp_ready", 2)
        b_done = signal("b_done", 2)
        t_ready = signal("t_ready", 2)
        a_ready = signal("a_ready", 2)
        sbo_done = signal("sbo_done", 2)
        mix_hi = signal("mix_hi", KC)
        mix_lo = signal("mix_lo", KC)
        rows_in = signal("rows_in", 2 * TOK)
        rows_tr = signal("rows_tr", TOK)
        qT_in = signal("qT_in", 2 + TOK)
        xs_done = signal("xs_done", X_HEADS)
        xnb = signal("xnb", X_HEADS)
        xe_done = signal("xe_done", X_HEADS)
        xp_ready = signal("xp_ready", X_HEADS)
        xp_tr = signal("xp_tr", X_HEADS)
        xpT_in = signal("xpT_in", X_HEADS)
        xo_done = signal("xo_done", X_HEADS)
        xo_hi = signal("xo_hi", X_HEADS)
        xo_lo = signal("xo_lo", X_HEADS)
        u_tr = signal("u_tr", 1)
        y_tap2 = signal("y_tap2", UP_TILES)
        y_conv = signal("y_conv", UP_TILES)
        gelu_done = signal("gelu_done", UP_TILES)
        gv_done = signal("gv_done", UP_TILES)
        g_hi = signal("g_hi", UP_TILES)
        g_lo = signal("g_lo", UP_TILES)
        zero_set = signal("zero_set", 0, before=1)
        half_set = signal("half_set", 0, before=1)
        dve_chain = ctx.enter_context(nc.semaphore("dve_chain"))
        act_chain = ctx.enter_context(nc.semaphore("act_chain"))
        out_done = signal("out_done", 0, before=TOK, unit=16)

        def st(i, n=1):
            return stat[:, i:i + n]

        S_HSQ, S_HMS, S_HRS, S_H0, S_YSQ, S_YMS, S_YRS, S_Y0, S_POW = 0, 4, 6, 8, 10, 14, 16, 18, 20
        S_MX, S_NB, S_DEN, S_RDEN = 24, 32, 40, 48
        S_BN, S_MV, S_LMS, S_LRS = 56, 68, 72, 74
        S_XMX, S_XNB, S_XDEN, S_XRD = 76, 80, 84, 88

        def chunks(buf, b, t):
            return buf[:, :].rearrange("p (c n) -> p c n", c=KC)[:, 4 * b:4 * b + 4, t * P:(t + 1) * P]

        def blocks(ps, n=4):
            return ps[:, 0:n * P].rearrange("p (c n) -> p c n", c=n)

        block = ctx.enter_context(nc.Block())


        @block.sync
        def _(sp_):
            x_by_tile = x.rearrange("(t p) n -> p t n", p=P)
            sp_.dma_start(cst[:, 0:CC_TRI], consts[:, 0:CC_TRI]).then_inc(head_in.sem, 16)
            sp_.dma_start(memn[:, 0:D], mem[0:P, :]).then_inc(mem0_in.sem, 16)
            sp_.dma_start(gpre[:, :], gains[0, MEM_G, :].partition_broadcast(P)).then_inc(mgain_in.sem, 16)
            sp_.dma_start(memn[:, D:2 * D], mem[P:2 * P, :]).then_inc(mem1_in.sem, 16)
            for s in range(2):
                sp_.dma_start(raw[:, s * GW:(s + 1) * GW], stream[s]).then_inc(raw_in[s].sem, 16)
            sp_.dma_start(h[:, :].rearrange("p (t n) -> p t n", t=TOK), x_by_tile).then_inc(x_in.sem, 16)
            for s in range(2, RING):
                sp_.dma_start(raw[:, s * GW:(s + 1) * GW], stream[s]).then_inc(raw_in[s].sem, 16)
            sp_.dma_start(cst[:, CC_TRI:CC], consts[:, CC_TRI:CC]).then_inc(cst_in.sem, 16)
            with sp_.Fori(1, DEPTH * GROUPS // RING) as r:
                for s in range(RING):
                    sp_.wait_ge(w_lo.sem, r * RING + (s + 1 - RING))
                    sp_.dma_start(raw[:, s * GW:(s + 1) * GW], stream[r * RING + s]).then_inc(raw_in[s].sem, 16)
            for s in range(RING):
                sp_.wait_ge(w_lo.sem, DEPTH * GROUPS + s + 1 - RING)
                sp_.dma_start(raw[:, s * GW:(s + 1) * GW], stream[s]).then_inc(raw_in[s].sem, 16)
            for t in range(TOK):
                sp_.wait_ge(h_ready.sem, h_ready.at(DEPTH, 2 * (t + 1) - 2 * TOK))
                sp_.dma_start(out[t * P:(t + 1) * P, :], h[:, t * D:(t + 1) * D]).then_inc(out_done.sem, 16)
            for s in range(RING):
                sp_.wait_ge(raw_in[s].sem, raw_in[s].at(DEPTH, 1))
            sp_.wait_ge(out_done.sem, out_done.at(0, 0))

        @block.gpsimd
        def _(pool):
            def gain(buf, landed, layer, row):
                pool.dma_start(buf[:, :], gains[layer, row, :].partition_broadcast(P)).then_inc(landed.sem, 16)

            def load_params(layer):
                pool.dma_start(par[:, :], params[layer]).then_inc(par_in.sem, 16)
                pool.dma_start(pww[:, :], pw[layer]).then_inc(par_in.sem, 16)

            def rsqrt(col_out, col_in):
                return pool.tensor_tensor(st(col_out), st(col_in), st(S_POW), ALU.pow)

            pool.dma_start(posi[:, :], pos).then_inc(pos_in.sem, 16)
            pool.memset(st(S_POW), -0.5).then_inc(half_set.sem, 1)
            gain(gpost, gpost_in, 0, MIX_POST)
            load_params(0)
            pool.wait_ge(half_set.sem, 1)
            for t in range(TOK):
                pool.wait_ge(mem_ms.sem, mem_ms.at(0, t - TOK + 1))
                rsqrt(S_HRS + t, S_HMS + t).then_inc(mem_rs.sem, 1)
            pool.wait_ge(mg_done.sem, mg_done.at(0, 0))
            gain(gpre, gpre_in, 0, MIX_PRE)

            def before_sub_layer(l, i, t):
                pool.wait_ge(h_ms.sem, h_ms.at(l, TOK * i + t + 1))
                rsqrt(S_HRS + t, S_HMS + t).then_inc(h_rs.sem, 1)

            for t in range(TOK):
                before_sub_layer(0, 0, t)

            with pool.Fori(0, DEPTH) as l:
                def turn(i):
                    for t in range(TOK):
                        pool.wait_ge(y_ms.sem, y_ms.at(l, TOK * i + t + 1))
                        rsqrt(S_YRS + t, S_YMS + t).then_inc(y_rs.sem, 1)
                        before_sub_layer(l, i + 1, t)

                pool.wait_ge(xn_ready.sem, xn_ready.at(l, 2 * TOK))
                gain(gpre, gpre_in, l, X_PRE)
                for t in range(TOK):
                    pool.wait_ge(ln_ms.sem, ln_ms.at(l, t + 1))
                    rsqrt(S_LRS + t, S_LMS + t).then_inc(ln_rs.sem, 1)
                turn(0)
                pool.wait_ge(h_ready.sem, h_ready.at(l, 2 * TOK))
                gain(gpost, gpost_in, l, X_POST)
                pool.wait_ge(xn_ready.sem, xn_ready.at(l, 4 * TOK))
                gain(gpre, gpre_in, l, FFN_PRE)
                turn(1)
                pool.wait_ge(h_ready.sem, h_ready.at(l, 4 * TOK))
                gain(gpost, gpost_in, l, FFN_POST)
                pool.wait_ge(xn_ready.sem, xn_ready.at(l, 6 * TOK))
                gain(gpre, gpre_in, l + 1, MEM_G)
                pool.wait_ge(mg_done.sem, mg_done.at(l, TOK))
                gain(gpre, gpre_in, l + 1, MIX_PRE)
                turn(2)
                pool.wait_ge(h_ready.sem, h_ready.at(l, 6 * TOK))
                gain(gpost, gpost_in, l + 1, MIX_POST)
                load_params(l + 1)
            pool.wait_ge(gpre_in.sem, gpre_in.at(DEPTH, 0))
            pool.wait_ge(gpost_in.sem, gpost_in.at(DEPTH, 0))
            pool.wait_ge(par_in.sem, par_in.at(DEPTH, 0))

        @block.scalar
        def _(act):
            own = Chain(act, act_chain)
            def memory_hi(l, t, n0=0):
                for b in range(2):
                    act.wait_ge(mt_tr.sem, mt_tr.at(l, n0 + 2 * t + b + 1))
                    act.activation(chunks(mT_hi, b, t), blocks(psCD[b]), ACT.Copy).then_inc(mt_hi.sem, 1)

            def split_group(l, g):
                s = g % RING
                act.wait_ge(raw_in[s].sem, raw_in[s].at(l, g // RING + 1))
                act.wait_ge(w_used.sem, w_used.at(l, g + 1 - RING))
                act.activation(whi[:, s * GW:(s + 1) * GW], raw[:, s * GW:(s + 1) * GW], ACT.Copy).then_inc(w_hi.sem, 1)

            def squares_h(l, i, t):
                for n in range(2):
                    cols = slice(t * D + n * NT, t * D + (n + 1) * NT)
                    act.wait_ge(h_ready.sem, h_ready.at(l, 2 * TOK * (i - 1) + 2 * t + n + 1))
                    act.activation(junk[:, cols], h[:, cols], ACT.Square, accum_out=st(S_HSQ + 2 * t + n)).then_inc(h_sq.sem, 1)

            for t, landed in enumerate((mem0_in, mem1_in)):
                act.wait_ge(landed.sem, 16)
                act.activation(junk[:, t * D:(t + 1) * D], memn[:, t * D:(t + 1) * D], ACT.Square,
                               accum_out=st(S_HSQ + t)).then_inc(mem_sq.sem, 1)
            act.wait_ge(trig_arg.sem, 1)
            act.activation(trig[:, :], trig[:, :], ACT.Sin).then_inc(trig_ready.sem, 1)
            split_group(0, 0)
            for t in range(TOK):
                memory_hi(0, t, -2 * TOK)
            split_group(0, 1)
            act.wait_ge(x_in.sem, 16)
            for t in range(TOK):
                squares_h(0, 0, t)
            for g in range(2, RING):
                split_group(0, g)

            with act.Fori(0, DEPTH) as l:
                split_to = [RING]

                def split(upto):
                    for g in range(split_to[0], upto + 1):
                        split_group(l, g)
                    split_to[0] = max(split_to[0], upto + 1)

                def square_y(t, n, bank_set):
                    act.activation(junk[:, t * D + n * NT:t * D + (n + 1) * NT], y_banks[bank_set][t],
                                   ACT.Square, accum_out=st(S_YSQ + 2 * t + n)).then_inc(y_sq.sem, 1)

                def squares_first(bank_set, g_end):
                    act.wait_ge(w_used.sem, w_used.at(l, g_end))
                    for t in range(TOK):
                        square_y(t, 0, bank_set)

                def turn(i, halves, g_end):
                    for n, bank_set, ready, _ in halves:
                        act.wait_ge(y_tile0.sem, y_tile0.at(l, ready))
                        square_y(0, n, bank_set)
                    split(g_end + 1)
                    squares_h(l, i + 1, 0)
                    if i == 0:
                        split(g_end + 2)
                    for n, bank_set, _, g in halves:
                        act.wait_ge(w_used.sem, w_used.at(l, g))
                        square_y(1, n, bank_set)
                    if i == 1:
                        input_hi(i + 1, 0)
                        split(g_end + 2)
                    else:
                        split(g_end + 3)
                        if i == 0:
                            input_hi(i + 1, 0)
                            split(g_end + 4)
                    squares_h(l, i + 1, 1)

                def input_hi(i, t):
                    for b in range(2):
                        act.wait_ge(xt_tr.sem, xt_tr.at(l, 2 * TOK * i + 2 * t + b + 1))
                        act.activation(chunks(xT_hi, b, t), blocks(psCD[b]), ACT.Copy).then_inc(xt_hi.sem, 1)

                def transposed_in(dst, src, g_end, arrived):
                    act.wait_ge(w_used.sem, w_used.at(l, g_end))
                    for b in range(2):
                        act.activation(dst[:, b * 2 * SEQ:(b + 1) * 2 * SEQ], src[b], ACT.Copy).then_inc(arrived.sem, 1)

                def v_rows(n, src, g_end):
                    act.wait_ge(w_used.sem, w_used.at(l, g_end))
                    for t in range(TOK):
                        act.activation(V[:, t * D + n * NT:t * D + (n + 1) * NT], src[t], ACT.Copy).then_inc(V_in.sem, 1)

                def exp_pair(c):
                    for r in range(2):
                        act.wait_ge(nb_ready.sem, nb_ready.at(l, 2 * c + r + 1))
                        for q, (a, b) in enumerate(((0, P), (P, AW))):
                            p = sms[c % 2][r][:, a:b]
                            e = act.activation(p, p, ACT.Exp, bias=st(S_NB + 4 * (c % 2) + 2 * r + q),
                                               scale=HD ** -0.5)
                        e.then_inc(exp_done.sem, 1)

                def scale_pair(c):
                    for r in range(2):
                        act.wait_ge(den_ready.sem, den_ready.at(l, 2 * c + r + 1))
                        for q, (a, b) in enumerate(((0, P), (P, AW))):
                            p = sms[c % 2][r][:, a:b]
                            e = act.activation(p, p, ACT.Copy, scale=st(S_RDEN + 4 * (c % 2) + 2 * r + q))
                        e.then_inc(p_ready.sem, 1)

                def p_columns(c):
                    for r in range(2):
                        act.wait_ge(p_tr.sem, p_tr.at(l, 2 * c + r + 1))
                        if c and not r:
                            act.wait_ge(o_done.sem, o_done.at(l, c))
                        act.activation(pT[:, r, :], psCD[r][:, 0:AW], ACT.Copy).then_inc(pT_in.sem, 1)

                def mixed_hi(chunk, ready, n, src, bias=None):
                    act.wait_ge(ready.sem, ready.at(l, n))
                    act.activation(oT_hi[:, chunk * SEQ:(chunk + 1) * SEQ], src,
                                   ACT.Copy if bias is None else ACT.Identity,
                                   bias=0.0 if bias is None else bias).then_inc(mix_hi.sem, 1)

                def softplus_pair(c):
                    act.wait_ge(zs_ready.sem, zs_ready.at(l, c + 1))
                    if c:
                        act.wait_ge(t_ready.sem, t_ready.at(l, c))
                    own.link(act.activation(sp, zs, ACT.Abs))
                    own.link(act.activation(sp, sp, ACT.Exp, scale=-1.0))
                    if c == 0:
                        p_columns(3)
                    act.activation(sp, sp, ACT.Ln, bias=1.0).then_inc(sp0_ready.sem, 1)

                def sb_weights(c):
                    act.wait_ge(t_ready.sem, t_ready.at(l, c + 1))
                    act.activation(sb_w[c], tt, ACT.Exp).then_inc(a_ready.sem, 1)

                input_hi(0, 0)
                split(6)
                transposed_in(KT[:, 0:4 * SEQ], psAB, G_WK0 + PER_TILE, KT_in)
                split(G_DLQ + PER_TILE - 1)
                input_hi(0, 1)
                split(G_CV + PER_TILE - 1 + AHEAD)
                act.wait_ge(w_used.sem, w_used.at(l, G_CV + PER_TILE))
                def columns(dst, ready, arrived):
                    for t in range(TOK):
                        act.wait_ge(ready.sem, ready.at(l, t + 1))
                        act.activation(dst[:, :, t * P:(t + 1) * P], blocks(psCD[t]), ACT.Copy).then_inc(arrived.sem, 1)

                act.activation(sig, accs[1][1][:, :], ACT.Sigmoid).then_inc(cv_sig.sem, 1)
                columns(dqT, q_tr, dqT_in)
                act.wait_ge(gpad_in.sem, gpad_in.at(l, 1))
                for c in range(2):
                    act.activation(cacc[:, c * SEQ:(c + 1) * SEQ], gpad[:, c, 0:SEQ], ACT.Identity,
                                   scale=par[:, PC_CVW + c * CV_K:PC_CVW + c * CV_K + 1],
                                   bias=par[:, PC_CVB + c:PC_CVB + c + 1]).then_inc(tap0.sem, 1)

                split(G_DLV + 1 + AHEAD)
                columns(dkT, kr_tr, dkT_in)
                split(G_DLV + 3 + AHEAD)
                act.wait_ge(w_used.sem, w_used.at(l, G_DLV + PER_TILE))
                for t in range(TOK):
                    act.activation(dlv[:, t * NT:(t + 1) * NT], accs[1][t][:, :], ACT.Copy).then_inc(dlv_in.sem, 1)
                split(G_SBQK + AHEAD)
                exp_pair(0)
                scale_pair(0)
                split(G_SBQK + 1 + AHEAD)
                exp_pair(1)
                split(G_SBQK + 2 + AHEAD)
                p_columns(0)
                scale_pair(1)
                exp_pair(2)
                split(G_SBQK + 3 + AHEAD)
                mixed_hi(4, o_done, 1, attended)
                p_columns(1)
                scale_pair(2)
                exp_pair(3)
                split(G_SBV + AHEAD)
                mixed_hi(5, o_done, 2, attended)
                p_columns(2)
                transposed_in(sbT.rearrange("p c n -> p (c n)"), [a[:, :] for a in accs[0]], G_SBQK + PER_TILE, sbT_in)
                scale_pair(3)
                mixed_hi(6, o_done, 3, attended)
                split(G_SBV + 1 + AHEAD)
                softplus_pair(0)
                act.wait_ge(w_used.sem, w_used.at(l, G_SBV + PER_TILE // 2))
                act.activation(sbv, accs[1][0][:, :], ACT.Copy).then_inc(sbv_in.sem, 1)
                split(G_WK1 + AHEAD)
                mixed_hi(7, o_done, 4, attended)
                split(G_WK1 + 2 + AHEAD)
                sb_weights(0)
                split(G_WK1 + 3 + AHEAD)
                softplus_pair(1)
                transposed_in(KT[:, 4 * SEQ:8 * SEQ], [a[:, :] for a in accs[0]], G_WK1 + PER_TILE, KT_in)
                split(G_WV0 + 1 + AHEAD)
                mixed_hi(0, sbo_done, 1, accs[0][0][:, 0:SEQ])
                split(G_WV0 + 2 + AHEAD)
                sb_weights(1)
                split(G_WV0 + 3 + AHEAD)
                mixed_hi(1, sbo_done, 2, psAB[1][:, 0:SEQ])
                for c in range(2):
                    act.wait_ge(ln_tb.sem, ln_tb.at(l, c + 1))
                    act.activation(sil[:, c * SEQ:(c + 1) * SEQ], psCD[c][:, 0:SEQ], ACT.Silu,
                                   scale=par[:, PC_LNG + c:PC_LNG + c + 1],
                                   bias=par[:, PC_LNB + c:PC_LNB + c + 1]).then_inc(silu.sem, 1)
                v_rows(0, [accs[1][t][:, :] for t in range(TOK)], G_WV0 + PER_TILE)
                split(G_OUT + AHEAD)
                for c in range(2):
                    mixed_hi(2 + c, pw_done, c + 1, psCD[c][:, 0:SEQ], par[:, PC_PWB + c:PC_PWB + c + 1])
                split(G_OUT + PER_TILE - 1 + AHEAD)
                squares_first(0, G_OUT + PER_TILE)
                split(G_OUT + 2 * PER_TILE - 1)
                turn(0, [(1, 1, 1, G_OUT + 2 * PER_TILE)], G_OUT + 2 * PER_TILE)

                split(G_WV1 + 3 + AHEAD)
                v_rows(1, psAB, G_WV1 + PER_TILE)
                split(G_XQ + PER_TILE - 1)
                input_hi(1, 1)

                def rows_out(i, g_end):
                    act.wait_ge(w_used.sem, w_used.at(l, g_end))
                    for t in range(TOK):
                        act.activation(rows[:, t * NT:(t + 1) * NT], accs[0][t][:, :], ACT.Copy).then_inc(rows_in.sem, 1)

                def exp_head(hd):
                    act.wait_ge(xnb.sem, xnb.at(l, hd + 1))
                    if hd >= 2:
                        act.wait_ge(xp_tr.sem, xp_tr.at(l, hd - 1))
                    for t in range(TOK):
                        e = act.activation(xp[:, hd % 2, t, :], psAB[hd % 2][:, t * SEQ:(t + 1) * SEQ], ACT.Exp,
                                           bias=st(S_XNB + 2 * (hd % 2) + t), scale=(D // X_HEADS) ** -0.5,
                                           accum_out=st(S_XDEN + 2 * (hd % 2) + t))
                    e.then_inc(xe_done.sem, 1)

                def xp_columns(hd):
                    act.wait_ge(xp_tr.sem, xp_tr.at(l, hd + 1))
                    if hd:
                        act.wait_ge(xo_done.sem, xo_done.at(l, hd))
                    act.activation(xpT, psCD[0][:, :], ACT.Copy).then_inc(xpT_in.sem, 1)

                def crossed_hi(hd):
                    act.wait_ge(xo_done.sem, xo_done.at(l, hd + 1))
                    act.activation(oT_hi[:, hd * 2 * SEQ:(hd + 1) * 2 * SEQ], psCD[1][:, :], ACT.Copy).then_inc(xo_hi.sem, 1)

                split(G_XQ + PER_TILE - 1 + AHEAD)
                rows_out(1, G_XQ + PER_TILE)
                split(G_XQ + PER_TILE + 1 + AHEAD)
                for t in range(TOK):
                    act.wait_ge(rows_tr.sem, rows_tr.at(l, t + 1))
                    act.activation(qT[:, 0:4, t * P:(t + 1) * P], blocks(psCD[t]), ACT.Copy).then_inc(qT_in.sem, 1)
                split(G_XQ + PER_TILE + 2 + AHEAD)
                exp_head(0)
                exp_head(1)
                split(G_XQ + 2 * PER_TILE - 1 + AHEAD)
                transposed_in(qT[:, 4:8, :].rearrange("p c n -> p (c n)"), [a[:, :] for a in accs[1]],
                              G_XQ + 2 * PER_TILE, qT_in)
                xp_columns(0)
                exp_head(2)
                crossed_hi(0)
                xp_columns(1)
                exp_head(3)
                split(G_XO + AHEAD)
                crossed_hi(1)
                xp_columns(2)
                split(G_XO + 2 + AHEAD)
                crossed_hi(2)
                xp_columns(3)
                split(G_XO + 4 + AHEAD)
                crossed_hi(3)
                turn(1, [(0, 0, 2, G_XO + 2 * PER_TILE - 2), (1, 1, 3, G_XO + 2 * PER_TILE)], G_XO + 2 * PER_TILE)
                split(G_UP + PER_TILE - 1)
                input_hi(2, 1)
                split(G_UP + PER_TILE - 1 + AHEAD)

                rows_out(2, G_UP + PER_TILE)

                def gate(j):
                    y = ffy[j % 2]
                    if j:
                        act.wait_ge(w_used.sem, w_used.at(l, G_UP + (j + 1) * PER_TILE))
                    else:
                        act.wait_ge(u_tr.sem, u_tr.at(l, 1))
                    if j >= 2:
                        act.wait_ge(gv_done.sem, gv_done.at(l, j - 1))
                    for c in range(4):
                        fc = (FFC if c >= 2 else 0) + 2 * j + c % 2
                        e = act.activation(y[:, c, :], up_chunk(j, c), ACT.Identity,
                                           scale=par[:, PC_FW + 3 * fc + 2:PC_FW + 3 * fc + 3],
                                           bias=par[:, PC_FB + fc:PC_FB + fc + 1])
                    e.then_inc(y_tap2.sem, 1)

                def gate_gelu(j):
                    act.wait_ge(y_conv.sem, y_conv.at(l, j + 1))
                    if j >= 2:
                        act.wait_ge(g_lo.sem, g_lo.at(l, j - 1))
                    act.activation(ffg[j % 2].rearrange("p (c n) -> p c n", c=2), ffy[j % 2][:, 0:2, :],
                                   ACT.Gelu_apprx_tanh).then_inc(gelu_done.sem, 1)
                    act.wait_ge(gv_done.sem, gv_done.at(l, j + 1))
                    act.activation(gT_hi[:, 2 * j * SEQ:2 * (j + 1) * SEQ], ffg[j % 2], ACT.Copy).then_inc(g_hi.sem, 1)

                for j in range(UP_TILES):
                    split(G_UP + (j + 1) * PER_TILE - 1 + AHEAD + (0 if j else 1))
                    gate(j)
                    split(G_UP + (j + 1) * PER_TILE + 1 + AHEAD)
                    gate_gelu(j)
                split(G_DOWN + 7 + AHEAD)
                memory_hi(l, 0)
                split(G_DOWN + 9 + AHEAD)
                memory_hi(l, 1)
                split(G_DOWN + DOWN_GROUPS - 1 + AHEAD)
                squares_first(2, G_DOWN + DOWN_GROUPS)
                split(GROUPS - 1)
                turn(2, [(1, 0, 4, GROUPS)], GROUPS)
                own.clear()

        @block.vector
        def _(dve):
            own = Chain(dve, dve_chain)

            dve.memset(zero[:, :].bitcast(F32), 0.0).then_inc(zero_set.sem, 1)

            def split_group(l, g):
                s = g % RING
                cols = slice(s * GW, (s + 1) * GW)
                dve.wait_ge(w_hi.sem, w_hi.at(l, g + 1))
                dve.tensor_tensor(wlo[:, cols], raw[:, cols], whi[:, cols].bitcast(F32), ALU.subtract).then_inc(w_lo.sem, 1)

            def mean_square(out_col, sq_col):
                return dve.tensor_scalar(st(out_col), st(sq_col), 1.0 / D, EPS, ALU.mult, ALU.add)

            scr = arena[:, 0:3 * TOK * 2 * HALF]
            ang, turns_ = scr[:, 0:TOK * 2 * HALF], scr[:, TOK * 2 * HALF:2 * TOK * 2 * HALF]
            posf = scr[:, 2 * TOK * 2 * HALF:2 * TOK * 2 * HALF + TOK]
            dve.wait_ge(head_in.sem, 16)
            dve.wait_ge(pos_in.sem, 16)
            own.link(dve.tensor_copy(posf, posi[:, :]))
            for t in range(TOK):
                for k in range(2):
                    e = dve.tensor_scalar(ang[:, (2 * t + k) * HALF:(2 * t + k + 1) * HALF],
                                          cst[:, CC_FRQ:CC_FRQ + HALF], posf[:, t:t + 1], None, ALU.mult)
            own.link(e)
            for t in range(TOK):
                for k in range(2):
                    cols = slice((2 * t + k) * HALF, (2 * t + k + 1) * HALF)
                    e = dve.tensor_scalar(turns_[:, cols], ang[:, cols], float(1 / (2 * np.pi)), 0.25 if k == 0 else 0.0,
                                          ALU.mult, ALU.add)
            own.link(e)
            nearest = 1.5 * 2.0 ** 23
            own.link(dve.tensor_scalar(turns_, turns_, nearest, -nearest, ALU.add, ALU.add))
            part1 = 6.28125
            part2 = float(np.float32(round((2 * np.pi - part1) * 2 ** 21) / 2 ** 21))
            part3 = float(2 * np.pi - part1 - part2)
            dve.wait_ge(mem_sq.sem, mem_sq.at(0, 1 - TOK))
            mean_square(S_HMS, S_HSQ).then_inc(mem_ms.sem, 1)
            for c in (part1, part2, part3):
                own.link(dve.scalar_tensor_tensor(ang, turns_, -c, ang, ALU.mult, ALU.add))
            for t in range(TOK):
                cols = slice(2 * t * HALF, (2 * t + 1) * HALF)
                e = dve.tensor_scalar(ang[:, cols], ang[:, cols], float(np.pi / 2), None, ALU.add)
            own.link(e)
            pi = 3.1415925
            dve.tensor_scalar(trig[:, :], ang, pi, -pi, ALU.min, ALU.max).then_inc(trig_arg.sem, 1)

            dve.wait_ge(mgain_in.sem, 16)
            for t in range(TOK):
                rows = slice(t * D, (t + 1) * D)
                dve.wait_ge(mem_rs.sem, mem_rs.at(0, t - TOK + 1))
                dve.scalar_tensor_tensor(xn[:, rows], memn[:, rows], st(S_HRS + t), gpre[:, :],
                                         ALU.mult, ALU.mult).then_inc(mg_done.sem, 1)
                if not t:
                    dve.wait_ge(mem_sq.sem, mem_sq.at(0, 0))
                    mean_square(S_HMS + 1, S_HSQ + 1).then_inc(mem_ms.sem, 1)
            def memory_gain():
                for t in range(TOK):
                    dve.tensor_tensor(xn[:, t * D:(t + 1) * D], memn[:, t * D:(t + 1) * D], gpre[:, :],
                                      ALU.mult).then_inc(mg_done.sem, 1)

            def memory_lo(l, t, n0=0):
                for b in range(2):
                    dve.wait_ge(mt_hi.sem, mt_hi.at(l, n0 + 2 * t + b + 1))
                    dve.tensor_tensor(chunks(mT_lo, b, t), blocks(psCD[b]), chunks(mT_hi, b, t).bitcast(F32),
                                      ALU.subtract).then_inc(mt_lo.sem, 1)

            memory_lo(0, 0, -2 * TOK)
            split_group(0, 0)
            memory_lo(0, 1, -2 * TOK)
            split_group(0, 1)
            for t in range(TOK):
                rows = slice(t * D, (t + 1) * D)
                dve.wait_ge(mg_done.sem, mg_done.at(0, t - TOK + 1))
                own.link(dve.tensor_scalar(memn[:, rows], memn[:, rows], st(S_HRS + t), None, ALU.mult))
            dve.wait_ge(x_in.sem, 16)
            for i in range(2 * TOK):
                dve.memset(st(S_HSQ + i), 0.0).then_inc(h_ready.sem, 1)
            def norm_input(l, i, t):
                dve.wait_ge(h_sq.sem, h_sq.at(l, 2 * TOK * i + 2 * (t + 1)))
                own.link(dve.tensor_scalar(st(S_H0 + t), st(S_HSQ + 2 * t), 1.0 / D, EPS, ALU.mult, ALU.add))
                dve.scalar_tensor_tensor(st(S_HMS + t), st(S_HSQ + 2 * t + 1), 1.0 / D, st(S_H0 + t),
                                         ALU.mult, ALU.add).then_inc(h_ms.sem, 1)

            def norm_scale(l, i, t, n_gain):
                dve.wait_ge(gpre_in.sem, gpre_in.at(l, n_gain))
                dve.wait_ge(h_rs.sem, h_rs.at(l, TOK * i + t + 1))
                for n in range(2):
                    cols = slice(t * D + n * NT, t * D + (n + 1) * NT)
                    dve.scalar_tensor_tensor(xn[:, cols], h[:, cols], st(S_HRS + t),
                                             gpre[:, n * NT:(n + 1) * NT], ALU.mult, ALU.mult).then_inc(xn_ready.sem, 1)

            for t in range(TOK):
                norm_input(0, 0, t)
                norm_scale(0, 0, t, 0)
                split_group(0, 2 + t)
            dve.wait_ge(trig_ready.sem, 1)
            own.clear()

            with dve.Fori(0, DEPTH) as l:
                split_to = [RING]

                def split(upto):
                    for g in range(split_to[0], upto + 1):
                        split_group(l, g)
                    split_to[0] = max(split_to[0], upto + 1)

                def input_lo(i, t):
                    for b in range(2):
                        dve.wait_ge(xt_hi.sem, xt_hi.at(l, 2 * TOK * i + 2 * t + b + 1))
                        dve.tensor_tensor(chunks(xT_lo, b, t), blocks(psCD[b]),
                                          chunks(xT_hi, b, t).bitcast(F32), ALU.subtract).then_inc(xt_lo.sem, 1)

                def output_gain(t, n, bank_set):
                    own.link(dve.tensor_tensor(xn[:, t * D + n * NT:t * D + (n + 1) * NT], y_banks[bank_set][t],
                                               gpost[:, n * NT:(n + 1) * NT], ALU.mult))

                def first_half(t):
                    own.link(dve.tensor_scalar(st(S_Y0 + t), st(S_YSQ + 2 * t), 1.0 / D, EPS, ALU.mult, ALU.add))

                def output_first(i, bank_set, g_end, n_gain):
                    dve.wait_ge(w_used.sem, w_used.at(l, g_end))
                    dve.wait_ge(gpost_in.sem, gpost_in.at(l, n_gain))
                    for t in range(TOK):
                        dve.wait_ge(y_sq.sem, y_sq.at(l, 2 * TOK * i + t + 1))
                        output_gain(t, 0, bank_set)
                    for t in range(TOK):
                        first_half(t)

                def turn(i, halves, g_end):
                    def output_rest(t):
                        for n, bank_set, counts in halves:
                            dve.wait_ge(y_sq.sem, y_sq.at(l, counts[t]))
                            if n:
                                dve.scalar_tensor_tensor(st(S_YMS + t), st(S_YSQ + 2 * t + 1), 1.0 / D,
                                                         st(S_Y0 + t), ALU.mult, ALU.add).then_inc(y_ms.sem, 1)
                            else:
                                first_half(t)
                            output_gain(t, n, bank_set)

                    n_gain = i + 1 if i < 2 else 4
                    output_rest(0)
                    split(g_end)
                    add_output(i, 0)
                    split(g_end + 1)
                    norm_input(l, i + 1, 0)
                    if i < 2:
                        norm_scale(l, i + 1, 0, n_gain)
                    if i == 0:
                        split(g_end + 2)
                    output_rest(1)
                    if i == 1:
                        input_lo(i + 1, 0)
                    add_output(i, 1)
                    if i == 2:
                        norm_scale(l, i + 1, 0, n_gain)
                        split(g_end + 2)
                        split(g_end + 3)
                    elif i == 1:
                        split(g_end + 2)
                    else:
                        split(g_end + 3)
                        input_lo(i + 1, 0)
                    norm_input(l, i + 1, 1)
                    if i == 0:
                        split(g_end + 4)
                    norm_scale(l, i + 1, 1, n_gain)

                def add_output(i, t):
                    dve.wait_ge(y_rs.sem, y_rs.at(l, TOK * i + t + 1))
                    for n in range(2):
                        cols = slice(t * D + n * NT, t * D + (n + 1) * NT)
                        dve.scalar_tensor_tensor(h[:, cols], xn[:, cols], st(S_YRS + t), h[:, cols],
                                                 ALU.mult, ALU.add).then_inc(h_ready.sem, 1)

                def rope(bank_set, dst, g_end, roped):
                    dve.wait_ge(w_used.sem, w_used.at(l, g_end))
                    for t in range(TOK):
                        if t:
                            dve.wait_ge(roped.sem, roped.at(l, t))
                        elif roped is k_roped:
                            dve.wait_ge(q_roped.sem, q_roped.at(l, TOK))
                        x3 = accs[bank_set][t][:, :].rearrange("p (g j) -> p g j", j=HALF)
                        a3 = ra.rearrange("p (g j) -> p g j", j=HALF)
                        b3 = rb.rearrange("p (g j) -> p g j", j=HALF)
                        cs = lambda k: trig[:, (2 * t + k) * HALF:(2 * t + k + 1) * HALF].unsqueeze(1)\
                            .to_broadcast([P, NT // HALF, HALF])
                        dve.tensor_tensor(a3, x3, cs(0), ALU.mult)
                        own.link(dve.tensor_tensor(b3, x3, cs(1), ALU.mult))
                        a4 = ra.rearrange("p (g r j) -> p g r j", r=2, j=HALF)
                        b4 = rb.rearrange("p (g r j) -> p g r j", r=2, j=HALF)
                        d4 = dst[:, t * NT:(t + 1) * NT].rearrange("p (g r j) -> p g r j", r=2, j=HALF)
                        dve.tensor_tensor(d4[:, :, 0], a4[:, :, 0], b4[:, :, 1], ALU.subtract)
                        dve.tensor_tensor(d4[:, :, 1], a4[:, :, 1], b4[:, :, 0], ALU.add).then_inc(roped.sem, 1)

                def scores_max(c):
                    w = 4 * (c % 2)
                    for r in range(2):
                        dve.wait_ge(s_done.sem, s_done.at(l, 2 * c + r + 1))
                        if c >= 2:
                            dve.wait_ge(p_tr.sem, p_tr.at(l, 2 * (c - 2) + r + 1))
                        own.link(dve.memset(st(S_MX + w + 2 * r, 2), -3e38))
                        for q, (a, b) in enumerate(((0, P), (P, AW))):
                            e = dve.tensor_tensor_reduce(sms[c % 2][r][:, a:b], psAB[r][:, a:b], negm[:, a:b], 1.0,
                                                         -3e38, ALU.add, ALU.max, st(S_MX + w + 2 * r + q))
                        own.link(e)
                        dve.tensor_scalar(st(S_NB + w + 2 * r, 2), st(S_MX + w + 2 * r, 2), -HD ** -0.5,
                                          None, ALU.mult).then_inc(nb_ready.sem, 1)

                def probabilities(c):
                    w = 4 * (c % 2)
                    for r in range(2):
                        dve.wait_ge(exp_done.sem, exp_done.at(l, 2 * c + r + 1))
                        for q, (a, b) in enumerate(((0, P), (P, AW))):
                            p = sms[c % 2][r][:, a:b]
                            e = dve.tensor_tensor_reduce(p, p, mult[:, a:b], 1.0, 0.0, ALU.mult, ALU.add,
                                                         st(S_DEN + w + 2 * r + q))
                        own.link(e)
                        dve.reciprocal(st(S_RDEN + w + 2 * r, 2), st(S_DEN + w + 2 * r, 2)).then_inc(den_ready.sem, 1)

                def mixed_lo(n, chunk, src, bias=None):
                    dve.wait_ge(mix_hi.sem, mix_hi.at(l, n))
                    cols = slice(chunk * SEQ, (chunk + 1) * SEQ)
                    if bias is None:
                        e = dve.tensor_tensor(oT_lo[:, cols], src, oT_hi[:, cols].bitcast(F32), ALU.subtract)
                    else:
                        e = dve.scalar_tensor_tensor(oT_lo[:, cols], src, bias, oT_hi[:, cols].bitcast(F32),
                                                     ALU.add, ALU.subtract)
                    e.then_inc(mix_lo.sem, 1)

                def conv_taps(lo, hi):
                    for j in range(lo, hi):
                        for c in range(2):
                            w = par[:, PC_CVW + c * CV_K + j:PC_CVW + c * CV_K + j + 1]
                            src, acc = gpad[:, c, j:j + SEQ], cacc[:, c * SEQ:(c + 1) * SEQ]
                            if j == 1:
                                dve.wait_ge(tap0.sem, tap0.at(l, c + 1))
                            else:
                                dve.wait_ge(own.sem, own.n - (0 if j == CV_K - 1 and c else 1))
                            e = dve.scalar_tensor_tensor(acc, src, w, acc, ALU.mult, ALU.add)
                            if j < CV_K - 1:
                                own.n += 1
                                e.then_inc(own.sem, 1)
                            else:
                                e.then_inc(conv_done.sem, 1)

                def sb_masked(c):
                    dve.wait_ge(z_done.sem, z_done.at(l, c + 1))
                    view = lambda a: a.rearrange("p (h n) -> p h n", h=2)
                    dve.scalar_tensor_tensor(view(zs), psA[:, :, 0:AW], HD ** -0.5, view(sbmask),
                                             ALU.mult, ALU.add).then_inc(zs_ready.sem, 1)

                def sb_keep(c):
                    dve.wait_ge(sp0_ready.sem, sp0_ready.at(l, c + 1))
                    dve.scalar_tensor_tensor(sp, zs, 0.0, sp, ALU.max, ALU.add).then_inc(sp_ready.sem, 1)

                def sb_between(c):
                    dve.wait_ge(b_done.sem, b_done.at(l, c + 1))
                    if c:
                        dve.wait_ge(a_ready.sem, a_ready.at(l, c))
                    view = lambda a: a.rearrange("p (h n) -> p h n", h=2)
                    dve.tensor_tensor(view(tt), psA[:, :, 0:AW], view(zs), ALU.add).then_inc(t_ready.sem, 1)

                input_lo(0, 0)
                split(G_DLQ + PER_TILE - 1)
                input_lo(0, 1)
                dve.wait_ge(par_in.sem, par_in.at(l, 0))
                dve.memset(gpad[:, :, 0:CV_K - 1], 0.0).then_inc(gpad_zero.sem, 1)
                split(G_DLQ + PER_TILE - 1 + AHEAD)
                rope(0, qr, G_DLQ + PER_TILE, q_roped)
                split(G_CV + PER_TILE - 1 + AHEAD)
                dve.wait_ge(cv_sig.sem, cv_sig.at(l, 1))
                dve.tensor_tensor(gpad[:, :, CV_K - 1:CV_K - 1 + SEQ],
                                  accs[1][0][:, :].rearrange("p (c n) -> p c n", c=2),
                                  sig.rearrange("p (c n) -> p c n", c=2), ALU.mult).then_inc(gpad_in.sem, 1)
                conv_taps(1, 4)
                split(G_DLK + AHEAD)
                conv_taps(4, 6)
                split(G_DLK + 1 + AHEAD)
                conv_taps(6, 8)
                split(G_DLK + 2 + AHEAD)
                conv_taps(8, 9)
                split(G_DLK + 3 + AHEAD)
                rope(0, kr, G_DLK + PER_TILE, k_roped)
                split(G_DLV + AHEAD)
                conv_taps(9, 11)
                split(G_DLV + 1 + AHEAD)
                conv_taps(11, 13)
                split(G_DLV + 2 + AHEAD)
                conv_taps(13, 15)
                split(G_DLV + 3 + AHEAD)
                dve.wait_ge(cst_in.sem, 16)
                scores_max(0)
                split(G_SBQK + AHEAD)
                probabilities(0)
                scores_max(1)
                split(G_SBQK + 1 + AHEAD)
                probabilities(1)
                scores_max(2)
                split(G_SBQK + 2 + AHEAD)
                conv_taps(15, 16)
                mixed_lo(1, 4, attended)
                probabilities(2)
                scores_max(3)
                split(G_SBQK + 3 + AHEAD)
                conv_taps(16, 17)
                mixed_lo(2, 5, attended)
                probabilities(3)
                conv_taps(17, 19)
                split(G_SBV + AHEAD)
                mixed_lo(3, 6, attended)
                sb_masked(0)
                conv_taps(19, 21)
                split(G_SBV + 1 + AHEAD)
                conv_taps(21, 23)
                sb_keep(0)
                split(G_WK1 + AHEAD)
                mixed_lo(4, 7, attended)
                split(G_WK1 + 1 + AHEAD)
                conv_taps(23, 25)
                sb_between(0)
                split(G_WK1 + 2 + AHEAD)
                conv_taps(25, 26)
                split(G_WK1 + 3 + AHEAD)
                sb_masked(1)
                conv_taps(26, 30)
                sb_keep(1)
                split(G_WV0 + AHEAD)
                conv_taps(30, CV_K)
                split(G_WV0 + 1 + AHEAD)
                mixed_lo(5, 0, accs[0][0][:, 0:SEQ])
                sb_between(1)
                for t in range(TOK):
                    dve.wait_ge(ln_tr.sem, ln_tr.at(l, t + 1))
                    own.link(dve.bn_stats(st(S_BN + 6 * t, 6), psCD[t][:, 0:CV_W]))
                    own.link(dve.bn_aggr(st(S_MV + 2 * t, 2), st(S_BN + 6 * t, 6)))
                    dve.tensor_scalar(st(S_LMS + t), st(S_MV + 2 * t + 1), EPS, None, ALU.add).then_inc(ln_ms.sem, 1)
                for t in range(TOK):
                    dve.wait_ge(ln_rs.sem, ln_rs.at(l, t + 1))
                    dve.tensor_scalar(lnn[:, t * CV_W:(t + 1) * CV_W], psCD[t][:, 0:CV_W], st(S_MV + 2 * t),
                                      st(S_LRS + t), ALU.subtract, ALU.mult).then_inc(ln_n.sem, 1)
                split(G_WV0 + 3 + AHEAD)
                mixed_lo(6, 1, psAB[1][:, 0:SEQ])
                split(G_OUT + AHEAD)
                for c in range(2):
                    mixed_lo(7 + c, 2 + c, psCD[c][:, 0:SEQ], par[:, PC_PWB + c:PC_PWB + c + 1])
                split(G_OUT + PER_TILE - 1 + AHEAD)
                output_first(0, 0, G_OUT + PER_TILE, 0)
                split(G_OUT + 2 * PER_TILE - 1)
                turn(0, [(1, 1, (3, 4))], G_OUT + 2 * PER_TILE)

                split(G_XQ + PER_TILE - 1)
                input_lo(1, 1)

                def cross_max(hd):
                    dve.wait_ge(xs_done.sem, xs_done.at(l, hd + 1))
                    b = hd % 2
                    own.link(dve.tensor_reduce(st(S_XMX + 2 * b, 2),
                                               psAB[b][:, :].rearrange("p (t n) -> p t n", t=TOK), AX_X, ALU.max))
                    dve.tensor_scalar(st(S_XNB + 2 * b, 2), st(S_XMX + 2 * b, 2), -(D // X_HEADS) ** -0.5, None,
                                      ALU.mult).then_inc(xnb.sem, 1)

                def cross_norm(hd):
                    dve.wait_ge(xe_done.sem, xe_done.at(l, hd + 1))
                    b = hd % 2
                    own.link(dve.reciprocal(st(S_XRD + 2 * b, 2), st(S_XDEN + 2 * b, 2)))
                    for t in range(TOK):
                        e = dve.tensor_scalar(xp[:, b, t, :], xp[:, b, t, :], st(S_XRD + 2 * b + t), None, ALU.mult)
                    e.then_inc(xp_ready.sem, 1)

                def crossed_lo(hd):
                    dve.wait_ge(xo_hi.sem, xo_hi.at(l, hd + 1))
                    cols = slice(hd * 2 * SEQ, (hd + 1) * 2 * SEQ)
                    dve.tensor_tensor(oT_lo[:, cols], psCD[1][:, :], oT_hi[:, cols].bitcast(F32),
                                      ALU.subtract).then_inc(xo_lo.sem, 1)

                split(G_XQ + PER_TILE + 2 + AHEAD)
                cross_max(0)
                cross_max(1)
                cross_norm(0)
                cross_norm(1)
                split(G_XQ + 2 * PER_TILE - 1 + AHEAD)
                cross_max(2)
                cross_norm(2)
                crossed_lo(0)
                cross_max(3)
                cross_norm(3)
                split(G_XO + AHEAD)
                crossed_lo(1)
                split(G_XO + 2 + AHEAD)
                crossed_lo(2)
                split(G_XO + 4 + AHEAD)
                crossed_lo(3)
                dve.wait_ge(gpost_in.sem, gpost_in.at(l, 1))
                turn(1, [(0, 0, (5, 7)), (1, 1, (6, 8))], G_XO + 2 * PER_TILE)
                split(G_UP + PER_TILE - 1)
                input_lo(2, 1)

                def up_taps(j):
                    y = ffy[j % 2]
                    dve.wait_ge(y_tap2.sem, y_tap2.at(l, j + 1))
                    for k in range(2):
                        for c in range(4):
                            fc = (FFC if c >= 2 else 0) + 2 * j + c % 2
                            u = up_chunk(j, c)
                            shift = k + 1
                            if k and c == 0:
                                dve.wait_ge(own.sem, own.n)
                            e = dve.scalar_tensor_tensor(y[:, c, shift:SEQ], u[:, 0:SEQ - shift],
                                                         par[:, PC_FW + 3 * fc + 1 - k:PC_FW + 3 * fc + 2 - k],
                                                         y[:, c, shift:SEQ], ALU.mult, ALU.add)
                            if k == 0 and c == 3:
                                own.n += 1
                                e.then_inc(own.sem, 1)
                    e.then_inc(y_conv.sem, 1)

                def gated(j):
                    y, g = ffy[j % 2], ffg[j % 2]
                    dve.wait_ge(gelu_done.sem, gelu_done.at(l, j + 1))
                    dve.tensor_tensor(g.rearrange("p (c n) -> p c n", c=2),
                                      g.rearrange("p (c n) -> p c n", c=2), y[:, 2:4, :], ALU.mult).then_inc(gv_done.sem, 1)

                def gated_lo(j):
                    cols = slice(2 * j * SEQ, 2 * (j + 1) * SEQ)
                    dve.wait_ge(g_hi.sem, g_hi.at(l, j + 1))
                    dve.tensor_tensor(gT_lo[:, cols], ffg[j % 2], gT_hi[:, cols].bitcast(F32), ALU.subtract).then_inc(g_lo.sem, 1)

                for j in range(UP_TILES):
                    split(G_UP + (j + 1) * PER_TILE - 1 + AHEAD + (0 if j else 1))
                    up_taps(j)
                    split(G_UP + (j + 1) * PER_TILE + 1 + AHEAD)
                    gated(j)
                    gated_lo(j)
                split(G_DOWN + 6 + AHEAD)
                dve.wait_ge(gpre_in.sem, gpre_in.at(l, 3))
                memory_gain()
                split(G_DOWN + 7 + AHEAD)
                memory_lo(l, 0)
                split(G_DOWN + 9 + AHEAD)
                memory_lo(l, 1)
                split(G_DOWN + DOWN_GROUPS - 1 + AHEAD)
                output_first(2, 2, G_DOWN + DOWN_GROUPS, 2)
                split(GROUPS - 1)
                turn(2, [(1, 0, (11, 12))], GROUPS)
                own.clear()

        @block.tensor
        def _(pe):
            pe.nop().then_inc(w_used.sem, RING)
            pe.wait_ge(head_in.sem, 16)
            pe.wait_ge(zero_set.sem, 1)

            def flip(dst, src, n=4):
                for i in range(n):
                    e = pe.transpose(dst[:, i * P:(i + 1) * P], src[:, i * P:(i + 1) * P], ident)
                return e

            def memory(l, t):
                pe.wait_ge(mg_done.sem, mg_done.at(l, t + 1))
                for b in range(2):
                    pe.wait_ge(mt_lo.sem, mt_lo.at(l, 2 * t + b - 1))
                    flip(psCD[b], xn[:, t * D + b * NT:t * D + (b + 1) * NT]).then_inc(mt_tr.sem, 1)

            for t in range(TOK):
                pe.wait_ge(mg_done.sem, mg_done.at(0, t - TOK + 1))
                for b in range(2):
                    if t:
                        pe.wait_ge(mt_lo.sem, mt_lo.at(0, b + 1 - 2 * TOK))
                    flip(psCD[b], xn[:, t * D + b * NT:t * D + (b + 1) * NT]).then_inc(mt_tr.sem, 1)
            pe.wait_ge(mt_lo.sem, mt_lo.at(0, 0))

            with pe.Fori(0, DEPTH) as l:
                def product(g0, groups, lhs, outs, k0=0, k_of=KC, width=NT, order=None):
                    hi, lo = lhs
                    per = GW // width
                    for g in range(g0, g0 + groups):
                        s = g % RING
                        pe.wait_ge(w_lo.sem, w_lo.at(l, g + 1))
                        for u in range(per):
                            k = k0 + (g - g0) * per + u
                            c = k if order is None else order[k]
                            cols = slice(s * GW + u * width, s * GW + (u + 1) * width)
                            for t in range(TOK):
                                a_hi = hi[:, c * SEQ + t * P:c * SEQ + (t + 1) * P]
                                a_lo = lo[:, c * SEQ + t * P:c * SEQ + (t + 1) * P]
                                pe.matmul(outs[t], a_hi, whi[:, cols], start=k == 0, stop=False)
                                pe.matmul(outs[t], a_hi, wlo[:, cols], start=False, stop=False)
                                e = pe.matmul(outs[t], a_lo, whi[:, cols], start=False, stop=k == k_of - 1)
                        e.then_inc(w_used.sem, 1)

                def open_bank(bank):
                    pe.matmul(bank, mT_hi[:, 0:P], zero[:, 0:1].to_broadcast([P, NT]), start=True, stop=False)

                def transposed_product(g0, groups, rhs, outs, k0=0, k_of=KC):
                    hi, lo = rhs
                    for g in range(g0, g0 + groups):
                        s = g % RING
                        pe.wait_ge(w_lo.sem, w_lo.at(l, g + 1))
                        for u in range(UNITS):
                            k = k0 + (g - g0) * UNITS + u
                            toks = slice(k * SEQ, (k + 1) * SEQ)
                            if k == 0 and len(outs) == 2:
                                for bank in outs:
                                    open_bank(bank)
                            for c in range(4):
                                cols = slice(s * GW + u * NT + c * P, s * GW + u * NT + (c + 1) * P)
                                dst = feature_chunk(outs, c)[:, 0:SEQ]
                                pe.matmul(dst, whi[:, cols], hi[:, toks], start=k == 0 and len(outs) == 4, stop=False)
                                pe.matmul(dst, whi[:, cols], lo[:, toks], start=False, stop=False)
                                e = pe.matmul(dst, wlo[:, cols], hi[:, toks], start=False,
                                              stop=k == KC - 1 and (c % 2 == 1 or len(outs) == 4))
                        e.then_inc(w_used.sem, 1)

                def feature_chunk(outs, c):
                    return outs[c] if len(outs) == 4 else outs[c // 2][:, c % 2 * SEQ:(c % 2 + 1) * SEQ]

                def first_product(i, g0, lhs, outs):
                    hi, lo = lhs
                    for t in range(TOK):
                        for g in range(g0, g0 + PER_TILE):
                            s = g % RING
                            if t == 0:
                                pe.wait_ge(w_lo.sem, w_lo.at(l, g + 1))
                                if g == g0 + PER_TILE - 1 and i < 2:
                                    inputs(i, 1)
                            if (g - g0) * UNITS % 4 == 0:
                                pe.wait_ge(xt_lo.sem, xt_lo.at(l, 2 * TOK * i + 2 * t + (g - g0) * UNITS // 4 + 1))
                            for u in range(UNITS):
                                k = (g - g0) * UNITS + u
                                cols = slice(s * GW + u * NT, s * GW + (u + 1) * NT)
                                a_hi = hi[:, k * SEQ + t * P:k * SEQ + (t + 1) * P]
                                a_lo = lo[:, k * SEQ + t * P:k * SEQ + (t + 1) * P]
                                pe.matmul(outs[t], a_hi, whi[:, cols], start=k == 0, stop=False)
                                pe.matmul(outs[t], a_hi, wlo[:, cols], start=False, stop=False)
                                e = pe.matmul(outs[t], a_lo, whi[:, cols], start=False, stop=k == KC - 1)
                            if t == TOK - 1:
                                e.then_inc(w_used.sem, 1)
                        if t == 0 and i == 2:
                            inputs(i, 1)

                def last_product(steps, lhs, k_of, order=None, heads_end=None):
                    hi, lo = lhs
                    for t in range(TOK):
                        for g, k0, outs, ends in steps if not t else sorted(steps):
                            if not t:
                                pe.wait_ge(w_lo.sem, w_lo.at(l, g + 1))
                                if heads_end == k0 + UNITS:
                                    pe.wait_ge(xo_lo.sem, xo_lo.at(l, X_HEADS))
                            s = g % RING
                            for u in range(UNITS):
                                c = k0 + u if order is None else order[k0 + u]
                                cols = slice(s * GW + u * NT, s * GW + (u + 1) * NT)
                                a_hi = hi[:, c * SEQ + t * P:c * SEQ + (t + 1) * P]
                                a_lo = lo[:, c * SEQ + t * P:c * SEQ + (t + 1) * P]
                                pe.matmul(acc[outs][t], a_hi, whi[:, cols], start=False, stop=False)
                                pe.matmul(acc[outs][t], a_hi, wlo[:, cols], start=False, stop=False)
                                e = pe.matmul(acc[outs][t], a_lo, whi[:, cols], start=False,
                                              stop=k0 + u == k_of - 1)
                            if t:
                                e.then_inc(w_used.sem, 1)
                            elif ends:
                                e.then_inc(y_tile0.sem, 1)

                X, O, M = (xT_hi, xT_lo), (oT_hi, oT_lo), (mT_hi, mT_lo)
                acc = [[accs[s][t][:, :] for t in range(TOK)] for s in range(2)]

                def inputs(i, t):
                    for b in range(2):
                        pe.wait_ge(xn_ready.sem, xn_ready.at(l, 2 * (TOK * i + t) + b + 1))
                        if t:
                            pe.wait_ge(xt_lo.sem, xt_lo.at(l, 2 * TOK * i + b + 1))
                        flip(psCD[b], xn[:, t * D + b * NT:t * D + (b + 1) * NT]).then_inc(xt_tr.sem, 1)

                def rows_to_columns(src, ready, n0, done, n=4):
                    for t in range(TOK):
                        pe.wait_ge(ready.sem, ready.at(l, n0 + t + 1))
                        flip(psCD[t], src[:, t * n * P:(t + 1) * n * P], n).then_inc(done.sem, 1)

                def dl_scores(c):
                    for r in range(2):
                        if c:
                            pe.wait_ge(nb_ready.sem, nb_ready.at(l, 2 * (c - 1) + r + 1))
                        q, k = (a[r * HD:(r + 1) * HD, c, :] for a in (dqT, dkT))
                        pe.matmul(psAB[r][:, 0:P], q[:, 0:P], k[:, 0:P], start=True, stop=True)
                        pe.matmul(psAB[r][:, P:AW], q[:, P:SEQ], k, start=True, stop=True).then_inc(s_done.sem, 1)

                def dl_flip(c):
                    for r in range(2):
                        pe.wait_ge(p_ready.sem, p_ready.at(l, 2 * c + r + 1))
                        flip(psCD[r], sms[c % 2][r], 3).then_inc(p_tr.sem, 1)

                def dl_values(c):
                    pe.wait_ge(pT_in.sem, pT_in.at(l, 2 * c + 2))
                    for r in range(2):
                        o, v0 = accs[1][1][r * HD:(r + 1) * HD, :], (2 * c + r) * HD
                        pe.matmul(o[:, 0:SEQ], dlv[:, v0:v0 + HD], pT[:, r, 0:SEQ], start=True, stop=False)
                        e = pe.matmul(o[:, P:SEQ], dlv[:, NT + v0:NT + v0 + HD], pT[:, r, SEQ:AW],
                                      start=False, stop=True)
                    e.then_inc(o_done.sem, 1)

                def sb_scores(c):
                    for r in range(2):
                        q, k = (sbT[r * HD:(r + 1) * HD, i + c, :] for i in (0, 2))
                        pe.matmul(psAB[r][:, 0:SEQ], k[:, 0:P], q, start=True, stop=True)
                        e = pe.matmul(psAB[r][:, SEQ:AW], k[:, P:SEQ], q[:, P:SEQ], start=True, stop=True)
                    e.then_inc(z_done.sem, 1)

                def sb_between(c):
                    pe.wait_ge(sp_ready.sem, sp_ready.at(l, c + 1))
                    for r in range(2):
                        k = sp[:, r * AW:(r + 1) * AW]
                        pe.matmul(psAB[r][:, 0:SEQ], tri, k[:, 0:SEQ], start=True, stop=False)
                        pe.matmul(psAB[r][:, P:SEQ], ones, k[:, SEQ:AW], start=False, stop=True)
                        e = pe.matmul(psAB[r][:, SEQ:AW], tri, k[:, SEQ:AW], start=True, stop=True)
                    e.then_inc(b_done.sem, 1)

                def sb_values(c, bank):
                    pe.wait_ge(a_ready.sem, a_ready.at(l, c + 1))
                    for r in range(2):
                        o, v0 = bank[r * HD:(r + 1) * HD, :], (2 * c + r) * HD
                        a = sb_w[c][:, r * AW:(r + 1) * AW]
                        pe.matmul(o[:, 0:SEQ], sbv[:, v0:v0 + HD], a[:, 0:SEQ], start=True, stop=False)
                        e = pe.matmul(o[:, P:SEQ], sbv[:, SB_W + v0:SB_W + v0 + HD], a[:, SEQ:AW],
                                      start=False, stop=True)
                    e.then_inc(sbo_done.sem, 1)

                transposed_product(G_WK0, 2, M, psAB)
                inputs(0, 0)
                transposed_product(G_WK0 + 2, 2, M, psAB, k0=4)
                first_product(0, G_DLQ, X, acc[0])
                transposed_product(G_CV, PER_TILE, X, acc[1])
                rows_to_columns(qr, q_roped, 0, q_tr)
                product(G_DLK, PER_TILE, X, acc[0])
                pe.wait_ge(gpad_in.sem, gpad_in.at(l, 1))
                pe.wait_ge(tap0.sem, tap0.at(l, 1))
                product(G_DLV, 2, X, acc[1])
                pe.wait_ge(dqT_in.sem, dqT_in.at(l, TOK))
                rows_to_columns(kr, k_roped, 0, kr_tr)
                product(G_DLV + 2, 2, X, acc[1], k0=4)
                pe.wait_ge(dkT_in.sem, dkT_in.at(l, TOK))
                pe.wait_ge(KT_in.sem, KT_in.at(l, 2))
                dl_scores(0)
                transposed_product(G_SBQK, 1, X, acc[0])
                dl_scores(1)
                transposed_product(G_SBQK + 1, 1, X, acc[0], k0=2)
                dl_flip(0)
                dl_scores(2)
                pe.wait_ge(dlv_in.sem, dlv_in.at(l, TOK))
                transposed_product(G_SBQK + 2, 1, X, acc[0], k0=4)
                dl_values(0)
                dl_flip(1)
                dl_scores(3)
                transposed_product(G_SBQK + 3, 1, X, acc[0], k0=6)
                pe.wait_ge(mix_lo.sem, mix_lo.at(l, 1))
                dl_values(1)
                dl_flip(2)

                def stick_values(t):
                    for g in range(G_SBV, G_SBV + PER_TILE // 2):
                        if not t:
                            pe.wait_ge(w_lo.sem, w_lo.at(l, g + 1))
                        for u in range(2 * UNITS):
                            k = (g - G_SBV) * 2 * UNITS + u
                            cols = slice(g % RING * GW + u * SB_W, g % RING * GW + (u + 1) * SB_W)
                            dst = accs[1][0][:, t * SB_W:(t + 1) * SB_W]
                            a_hi = xT_hi[:, k * SEQ + t * P:k * SEQ + (t + 1) * P]
                            a_lo = xT_lo[:, k * SEQ + t * P:k * SEQ + (t + 1) * P]
                            pe.matmul(dst, a_hi, whi[:, cols], start=k == 0, stop=False)
                            pe.matmul(dst, a_hi, wlo[:, cols], start=False, stop=False)
                            e = pe.matmul(dst, a_lo, whi[:, cols], start=False, stop=k == KC - 1)
                        if t:
                            e.then_inc(w_used.sem, 1)

                stick_values(0)
                pe.wait_ge(mix_lo.sem, mix_lo.at(l, 2))
                dl_values(2)
                pe.wait_ge(nb_ready.sem, nb_ready.at(l, DL_HEADS))
                pe.wait_ge(sbT_in.sem, sbT_in.at(l, 2))
                sb_scores(0)
                stick_values(1)
                dl_flip(3)
                transposed_product(G_WK1, 1, M, acc[0])
                pe.wait_ge(mix_lo.sem, mix_lo.at(l, 3))
                dl_values(3)
                transposed_product(G_WK1 + 1, 1, M, acc[0], k0=2)
                pe.wait_ge(cst_in.sem, 16)
                sb_between(0)
                transposed_product(G_WK1 + 2, 1, M, acc[0], k0=4)
                pe.wait_ge(t_ready.sem, t_ready.at(l, 1))
                sb_scores(1)
                transposed_product(G_WK1 + 3, 1, M, acc[0], k0=6)
                pe.wait_ge(sbv_in.sem, sbv_in.at(l, 1))
                pe.wait_ge(mix_lo.sem, mix_lo.at(l, 4))
                product(G_WV0, 2, M, acc[1])
                pe.wait_ge(KT_in.sem, KT_in.at(l, 4))
                sb_values(0, accs[0][0])
                sb_between(1)
                for t in range(TOK):
                    for c in range(2):
                        pe.wait_ge(conv_done.sem, conv_done.at(l, c + 1))
                        e = pe.transpose(psCD[t][:, c * P:(c + 1) * P],
                                         cacc[:, c * SEQ + t * P:c * SEQ + (t + 1) * P], ident)
                    e.then_inc(ln_tr.sem, 1)
                product(G_WV0 + 2, 2, M, acc[1], k0=4)
                sb_values(1, psAB[1])
                pe.wait_ge(ln_n.sem, ln_n.at(l, TOK))
                for c in range(2):
                    for t in range(TOK):
                        e = pe.transpose(psCD[c][:, t * P:(t + 1) * P], lnn[:, t * CV_W + c * P:t * CV_W + (c + 1) * P],
                                         ident)
                    e.then_inc(ln_tb.sem, 1)
                pe.wait_ge(mix_lo.sem, mix_lo.at(l, 5))
                product(G_OUT, 1, O, acc[0], order=MIX_ORDER)
                pe.wait_ge(silu.sem, silu.at(l, 2))
                for co in range(2):
                    for ci in range(2):
                        e = pe.matmul(psCD[co][:, 0:SEQ], pww[:, ci * CV_W + co * P:ci * CV_W + (co + 1) * P],
                                      sil[:, ci * SEQ:(ci + 1) * SEQ], start=ci == 0, stop=ci == 1)
                    e.then_inc(pw_done.sem, 1)
                product(G_OUT + 1, 1, O, acc[0], k0=2, order=MIX_ORDER)
                pe.wait_ge(mix_lo.sem, mix_lo.at(l, 6))
                product(G_OUT + 2, 1, O, acc[0], k0=4, order=MIX_ORDER)
                pe.wait_ge(mix_lo.sem, mix_lo.at(l, KC))
                product(G_OUT + 3, 1, O, acc[0], k0=6, order=MIX_ORDER)
                pe.wait_ge(V_in.sem, V_in.at(l, TOK))
                product(G_OUT + PER_TILE, 1, O, acc[1], order=MIX_ORDER)
                last_product([(G_OUT + PER_TILE + j, 2 * j, 1, j == 3) for j in range(1, 4)], O, KC, MIX_ORDER)
                product(G_WV1, 2, M, psAB)
                inputs(1, 0)
                product(G_WV1 + 2, 2, M, psAB, k0=4)

                def x_scores(hd):
                    if hd >= 2:
                        pe.wait_ge(xe_done.sem, xe_done.at(l, hd - 1))
                    for t in range(TOK):
                        for i in range(2):
                            e = pe.matmul(psAB[hd % 2][:, t * SEQ:(t + 1) * SEQ], qT[:, 2 * hd + i, t * P:(t + 1) * P],
                                          KT[:, (2 * hd + i) * SEQ:(2 * hd + i + 1) * SEQ], start=i == 0, stop=i == 1)
                    e.then_inc(xs_done.sem, 1)

                def x_flip(hd):
                    pe.wait_ge(xp_ready.sem, xp_ready.at(l, hd + 1))
                    for m in range(2):
                        for t in range(TOK):
                            e = pe.transpose(psCD[0][:, m * SEQ + t * P:m * SEQ + (t + 1) * P],
                                             xp[:, hd % 2, t, m * P:(m + 1) * P], ident)
                    e.then_inc(xp_tr.sem, 1)

                def x_values(hd):
                    pe.wait_ge(xpT_in.sem, xpT_in.at(l, hd + 1))
                    if hd:
                        pe.wait_ge(xo_lo.sem, xo_lo.at(l, hd))
                    for i in range(2):
                        for m in range(2):
                            v0 = m * D + (2 * hd + i) * P
                            e = pe.matmul(psCD[1][:, i * SEQ:(i + 1) * SEQ], V[:, v0:v0 + P],
                                          xpT[:, m * SEQ:(m + 1) * SEQ], start=m == 0, stop=m == 1)
                    e.then_inc(xo_done.sem, 1)

                first_product(1, G_XQ, X, acc[0])
                transposed_product(G_XQ + PER_TILE, 2, X, acc[1])
                rows_to_columns(rows, rows_in, 0, rows_tr)
                transposed_product(G_XQ + PER_TILE + 2, 1, X, acc[1], k0=4)
                pe.wait_ge(qT_in.sem, qT_in.at(l, TOK))
                pe.wait_ge(V_in.sem, V_in.at(l, 2 * TOK))
                x_scores(0)
                x_scores(1)
                transposed_product(G_XQ + PER_TILE + 3, 1, X, acc[1], k0=6)
                x_flip(0)
                pe.wait_ge(qT_in.sem, qT_in.at(l, TOK + 2))
                x_scores(2)
                x_values(0)
                x_flip(1)
                x_scores(3)

                def wo(hd, n):
                    product(G_XO + 2 * hd + n, 1, O, acc[n], k0=2 * hd)

                pe.wait_ge(xo_lo.sem, xo_lo.at(l, 1))
                wo(0, 0)
                x_values(1)
                x_flip(2)
                wo(0, 1)
                pe.wait_ge(xo_lo.sem, xo_lo.at(l, 2))
                wo(1, 0)
                x_values(2)
                x_flip(3)
                wo(1, 1)
                pe.wait_ge(xo_lo.sem, xo_lo.at(l, 3))
                x_values(3)
                g = G_XO + PER_TILE
                last_product([(g, 4, 0, False), (g + 2, 4, 1, False), (g + 1, 6, 0, True), (g + 3, 6, 1, True)], O, KC,
                             heads_end=KC)
                inputs(2, 0)

                for j in range(UP_TILES):
                    if j >= 2:
                        pe.wait_ge(y_conv.sem, y_conv.at(l, j - 1))
                    if j == 0:
                        first_product(2, G_UP, X, acc[0])
                    elif j == 1:
                        transposed_product(G_UP + PER_TILE, 1, X, up_banks[1])
                        for t in range(TOK):
                            pe.wait_ge(rows_in.sem, rows_in.at(l, TOK + t + 1))
                            for c in range(4):
                                e = pe.transpose(up_chunk(0, c)[:, t * P:(t + 1) * P],
                                                 rows[:, t * NT + c * P:t * NT + (c + 1) * P], ident)
                        e.then_inc(u_tr.sem, 1)
                        transposed_product(G_UP + PER_TILE + 1, 3, X, up_banks[1], k0=2)
                    else:
                        transposed_product(G_UP + j * PER_TILE, PER_TILE, X, up_banks[j % 2])
                G = (gT_hi, gT_lo)
                pe.wait_ge(y_conv.sem, y_conv.at(l, UP_TILES - 1))
                for g in range(DOWN_GROUPS):
                    pe.wait_ge(g_lo.sem, g_lo.at(l, g + 1))
                    product(G_DOWN + g, 1, G, psAB, k0=2 * g, k_of=FFC)
                    if g == 7:
                        memory(l, 0)
                    if g == 9:
                        memory(l, 1)
                g, last = G_DOWN + DOWN_GROUPS, DOWN_GROUPS - RING
                pe.wait_ge(y_conv.sem, y_conv.at(l, UP_TILES))
                product(g, last, G, acc[0], k_of=FFC)
                last_product([(g + j, 2 * j, 0, j == DOWN_GROUPS - 1) for j in range(last, DOWN_GROUPS)], G, FFC)

    return nc


def _weight_groups(a):
    def tiles(w, width=NT):
        k, n = w.shape
        per = GW // width
        v = w.reshape(k // P // per, per, P, n // width, width)
        return v.transpose(3, 0, 2, 1, 4).reshape(-1, P, GW)

    layers = []
    for l in range(DEPTH):
        w_in = a["w_in"][l]
        cv = 3 * SB_W
        dl = cv + 2 * CV_W
        k, v = tiles(a["x_wk"][l]), tiles(a["x_wv"][l])
        up = a["ffn_w_up"][l].reshape(D, 2, FFC // 2, 2 * P).transpose(0, 2, 1, 3).reshape(D, 2 * D_FF)
        w_out = a["w_out"][l].reshape(KC, P, D)[list(MIX_ORDER)].reshape(D, D)
        wo = tiles(a["x_wo"][l])[[0, 4, 1, 5, 2, 3, 6, 7]]
        layers += [k[:PER_TILE], tiles(w_in[:, dl:dl + NT]), tiles(w_in[:, cv:dl]),
                   tiles(w_in[:, dl + NT:]), tiles(w_in[:, 0:2 * SB_W]),
                   tiles(w_in[:, 2 * SB_W:cv], SB_W), k[PER_TILE:], v[:PER_TILE], tiles(w_out),
                   v[PER_TILE:], tiles(a["x_wq"][l]), wo, tiles(up), tiles(a["ffn_w_down"][l])]
    return np.ascontiguousarray(np.concatenate(layers))


def _by_feature(v, n):
    v = v.reshape(-1, n, P)
    return v.transpose(2, 1, 0).reshape(P, -1)


def _params(a):
    rows = []
    for l in list(range(DEPTH)) + [0]:
        rows.append(np.concatenate([
            _by_feature(a["cv_w"][l], 2), _by_feature(a["cv_b"][l], 2), _by_feature(a["cv_ln_g"][l], 2),
            _by_feature(a["cv_ln_b"][l], 2), _by_feature(a["cv_pw_b"][l], 2),
            _by_feature(a["ffn_conv_w"][l], 2 * FFC), _by_feature(a["ffn_conv_b"][l], 2 * FFC)], axis=1))
    return np.stack(rows)


def _gains(a):
    names = ["mem_norm", "mix_norm_pre", "mix_norm_post", "x_norm_pre", "x_norm_post", "ffn_norm_pre",
             "ffn_norm_post"]
    g = np.stack([a[n] for n in names], axis=1)
    return np.concatenate([g, g[:1]])


def _constants():
    c = np.zeros((P, CC), np.float32)
    i, j = np.arange(P)[:, None], np.arange(P)[None, :]
    c[:, CC_ID:CC_ID + P] = i == j
    c[:, CC_TRI:CC_TRI + P] = -(i >= j).astype(np.float32)
    c[:, CC_ONE:CC_ONE + P] = -1.0
    before = np.concatenate([np.arange(SEQ)[None, :] > i, j > i], axis=1)
    c[:, CC_SB:CC_SB + 2 * AW] = np.where(np.concatenate([before, before], axis=1), 0.0, -3e38)
    dist = np.concatenate([i - j, i + P - np.arange(SEQ)[None, :]], axis=1)
    count = sum(((dist >= 0) & (dist % d == 0) & (dist <= w)).astype(np.float32)
                for w, d in ((128, 1), (512, 4), (2048, 16)))
    c[:, CC_NEG:CC_NEG + AW] = np.where(count > 0, 0.0, -3e38)
    c[:, CC_MUL:CC_MUL + AW] = count
    c[:, CC_FRQ:CC_FRQ + HALF] = np.float32(10000.0) ** (-np.arange(HALF, dtype=np.float32) / np.float32(HALF))
    return c


def kernel(**inputs):
    import concourse.bacc as bacc
    from concourse.bass_utils import run_bass_kernel_spmd

    a = {k: np.asarray(v) for k, v in inputs.items()}
    arrays = {
        "x_dram": a["x"][0], "mem_dram": a["mem"][0],
        "pos_dram": a["positions"].reshape(TOK, P).T,
        "const_dram": _constants(), "gain_dram": _gains(a), "param_dram": _params(a),
        "pw_dram": np.concatenate([a["cv_pw_w"], a["cv_pw_w"][:1]])
                     .reshape(DEPTH + 1, 2, P, CV_W).transpose(0, 2, 1, 3).reshape(DEPTH + 1, P, 2 * CV_W),
        "stream_dram": _weight_groups(a),
    }
    arrays = {k: np.ascontiguousarray(v) for k, v in arrays.items()}
    nc = bacc.Bacc("TRN2", target_bir_lowering=False, num_devices=1)
    aps = [nc.dram_tensor(n, v.shape, mybir.dt.from_np(v.dtype), kind="ExternalInput").ap()
           for n, v in arrays.items()]
    out = nc.dram_tensor("out_dram", (SEQ, D), F32, kind="ExternalOutput").ap()
    hybrid_trunk(nc, *aps, out)
    r = run_bass_kernel_spmd(nc, [arrays], core_ids=[0])
    return r.results[0]["out_dram"].reshape(1, SEQ, D)
```
